# Optimizing a Trainium2 kernel written in Bass

```python
import math
import jax, jax.numpy as jnp
from jax import lax
import numpy as np

D_MODEL = 1024
BATCH = 1
SEQ = 1024
DEPTH = 1

D_MIX = D_MODEL
S5_WIDTH = D_MIX // 2
S5_GROUP = 16
S5_GROUPS = S5_WIDTH // S5_GROUP
S5_STATE = 64
ML_WIDTH = D_MIX - S5_WIDTH
ML_HEADS = 4
ML_HEAD_DIM = ML_WIDTH // ML_HEADS
ML_CHUNK = 64
CONV_WIDTH = 4
D_IN = S5_WIDTH + 4 * ML_WIDTH + 2 * ML_HEADS
N_EXPERTS = 32
TOP_K = 4
D_FF = D_MODEL
SWIGLU_LIMIT = 7.0
SWIGLU_ALPHA = 1.702
MOE_BLOCK = 128
RMS_EPS = 1e-5
LN_EPS = 1e-6

kernel_name = "hymba_s5_mlstm_moe_block"

def rmsnorm(x, g):
    xf = x.astype(jnp.float32)
    y = xf * lax.rsqrt(jnp.mean(xf * xf, axis=-1, keepdims=True) + RMS_EPS)
    return (y * g.astype(jnp.float32)).astype(x.dtype)

def s5_mixer(u, log_dt, a_re, a_im, b_re, b_im, c_re, c_im, d_skip, w_glu, b_glu):
    f32 = jnp.float32
    bsz, seq, _ = u.shape
    uf = u.astype(f32).reshape(bsz, seq, S5_GROUPS, S5_GROUP)
    a = lax.complex(jnp.minimum(a_re.astype(f32), -1e-4), a_im.astype(f32))
    dt = jnp.exp(log_dt.astype(f32))[:, None]
    a_bar = jnp.exp(dt * a)
    b_mat = lax.complex(b_re.astype(f32), b_im.astype(f32))
    b_bar = ((a_bar - 1.0) / a)[..., None] * b_mat
    c_mat = lax.complex(c_re.astype(f32), c_im.astype(f32))
    bu = jnp.einsum('gnp,bsgp->bsgn', b_bar, uf.astype(jnp.complex64))
    a_seq = jnp.broadcast_to(a_bar, (1, seq, S5_GROUPS, S5_STATE))

    def combine(left, right):
        a_l, x_l = left
        a_r, x_r = right
        return a_r * a_l, a_r * x_l + x_r

    _, states = lax.associative_scan(combine, (a_seq, bu), axis=1)
    y = jnp.einsum('gpn,bsgn->bsgp', c_mat, states).real \
        + d_skip.astype(f32).reshape(S5_GROUPS, S5_GROUP) * uf
    y = y.reshape(bsz, seq, S5_WIDTH)
    g = jax.nn.gelu(y)
    out = g * jax.nn.sigmoid(g @ w_glu.astype(f32) + b_glu.astype(f32))
    return out.astype(u.dtype)

def causal_conv(x, w, b):
    seq = x.shape[1]
    xp = jnp.pad(x, ((0, 0), (CONV_WIDTH - 1, 0), (0, 0)))
    out = b
    for j in range(CONV_WIDTH):
        out = out + w[j] * xp[:, j:j + seq]
    return out

def mlstm_chunkwise(q, k, v, i_pre, f_pre):
    bsz, nh, seq, dh = q.shape
    nc = seq // ML_CHUNK
    L = ML_CHUNK

    def to_chunks(t):
        return jnp.moveaxis(t.reshape(bsz, nh, nc, L, *t.shape[3:]), 2, 0)

    qc = to_chunks(q)
    kc = to_chunks(k * (1.0 / math.sqrt(dh)))
    vc = to_chunks(v)
    ic = to_chunks(i_pre)
    lfc = to_chunks(jax.nn.log_sigmoid(f_pre))
    causal = jnp.tril(jnp.ones((L, L), dtype=bool))

    def step(carry, inp):
        c_prev, n_prev, m_prev = carry
        q_c, k_c, v_c, i_c, lf_c = inp
        b = jnp.cumsum(lf_c, axis=-1)
        log_d = jnp.where(causal, b[..., :, None] - b[..., None, :] + i_c[..., None, :], -jnp.inf)
        log_inter = b + m_prev[..., None]
        m = jnp.maximum(log_inter, jnp.max(log_d, axis=-1))
        w_intra = jnp.exp(log_d - m[..., None])
        w_inter = jnp.exp(log_inter - m)
        s = jnp.einsum('bhtd,bhsd->bhts', q_c, k_c) * w_intra
        num = w_inter[..., None] * jnp.einsum('bhtd,bhde->bhte', q_c, c_prev) \
            + jnp.einsum('bhts,bhse->bhte', s, v_c)
        den = w_inter * jnp.einsum('bhtd,bhd->bht', q_c, n_prev) + jnp.sum(s, axis=-1)
        h = num / jnp.maximum(jnp.abs(den), jnp.exp(-m))[..., None]
        b_last = b[..., -1]
        log_w_state = b_last[..., None] - b + i_c
        m_next = jnp.maximum(b_last + m_prev, jnp.max(log_w_state, axis=-1))
        decay = jnp.exp(b_last + m_prev - m_next)
        w_state = jnp.exp(log_w_state - m_next[..., None])
        c_next = decay[..., None, None] * c_prev + jnp.einsum('bhs,bhsd,bhse->bhde', w_state, k_c, v_c)
        n_next = decay[..., None] * n_prev + jnp.einsum('bhs,bhsd->bhd', w_state, k_c)
        return (c_next, n_next, m_next), h

    init = (jnp.zeros((bsz, nh, dh, dh), jnp.float32),
            jnp.zeros((bsz, nh, dh), jnp.float32),
            jnp.zeros((bsz, nh), jnp.float32))
    _, hs = lax.scan(step, init, (qc, kc, vc, ic, lfc))
    return jnp.moveaxis(hs, 0, 2).reshape(bsz, nh, seq, dh)

def mlstm_mixer(q_pre, k_pre, v, o_pre, gate_pre, conv_w, conv_b, b_gates, norm_g):
    f32 = jnp.float32
    bsz, seq, _ = v.shape
    qk = jnp.concatenate([q_pre, k_pre], axis=-1).astype(f32)
    qk = jax.nn.silu(causal_conv(qk, conv_w.astype(f32), conv_b.astype(f32)))
    q, k = jnp.split(qk, 2, axis=-1)

    def heads(t):
        return t.reshape(bsz, seq, ML_HEADS, ML_HEAD_DIM).transpose(0, 2, 1, 3)

    gates = (gate_pre.astype(f32) + b_gates.astype(f32)).transpose(0, 2, 1)
    i_pre, f_pre = gates[:, :ML_HEADS], gates[:, ML_HEADS:]
    h = mlstm_chunkwise(heads(q), heads(k), heads(v.astype(f32)), i_pre, f_pre)
    mu = jnp.mean(h, axis=-1, keepdims=True)
    var = jnp.mean(jnp.square(h - mu), axis=-1, keepdims=True)
    h = (h - mu) * lax.rsqrt(var + LN_EPS)
    h = h.transpose(0, 2, 1, 3).reshape(bsz, seq, ML_WIDTH) * norm_g.astype(f32)
    out = h * jax.nn.sigmoid(o_pre.astype(f32))
    return out.astype(v.dtype)

def moe_ffn(x, w_router, b_router, w_up, b_up, w_down, b_down):
    bsz, seq, d = x.shape
    t = x.reshape(-1, d)
    n_tok = t.shape[0]
    logits = (t @ w_router + b_router).astype(jnp.float32)
    top_vals, top_idx = lax.top_k(logits, TOP_K)
    gate = jax.nn.softmax(top_vals, axis=-1)
    n_assign = n_tok * TOP_K
    flat_e = top_idx.reshape(-1)
    order = jnp.argsort(flat_e)
    sorted_e = flat_e[order]
    sorted_tok = (order // TOP_K).astype(jnp.int32)
    sorted_gate = gate.reshape(-1)[order]
    counts = jnp.bincount(flat_e, length=N_EXPERTS)
    start = jnp.cumsum(counts) - counts
    padded = (counts + MOE_BLOCK - 1) // MOE_BLOCK * MOE_BLOCK
    pad_end = jnp.cumsum(padded)
    pad_start = pad_end - padded
    dest = pad_start[sorted_e] + (jnp.arange(n_assign) - start[sorted_e])
    n_slots = (n_assign + MOE_BLOCK - 1) // MOE_BLOCK * MOE_BLOCK + N_EXPERTS * MOE_BLOCK
    n_blocks = n_slots // MOE_BLOCK
    slot_tok = jnp.zeros((n_slots,), jnp.int32).at[dest].set(sorted_tok)
    block_start = jnp.arange(n_blocks) * MOE_BLOCK
    block_e = jnp.minimum(jnp.sum(pad_end[None, :] <= block_start[:, None], axis=-1), N_EXPERTS - 1)
    xs = t[slot_tok].reshape(n_blocks, MOE_BLOCK, d)

    def expert_block(args):
        xb, e = args
        h = xb @ w_up[e] + b_up[e]
        g = jnp.minimum(h[:, :D_FF], SWIGLU_LIMIT)
        lin = jnp.clip(h[:, D_FF:], -SWIGLU_LIMIT, SWIGLU_LIMIT)
        act = g * jax.nn.sigmoid(SWIGLU_ALPHA * g) * (lin + 1.0)
        return act @ w_down[e] + b_down[e]

    ys = lax.map(expert_block, (xs, block_e)).reshape(n_slots, d)
    y_assign = ys[dest].astype(jnp.float32) * sorted_gate[:, None]
    y = jax.ops.segment_sum(y_assign, sorted_tok, num_segments=n_tok)
    return y.reshape(bsz, seq, d).astype(x.dtype)

def setup_inputs(seed: int = 0) -> dict:
    key = jax.random.key(seed)
    ks = jax.random.split(key, 28)
    nrm = jax.random.normal
    f32 = jnp.float32
    L_ = DEPTH
    x = nrm(ks[0], (BATCH, SEQ, D_MODEL), f32)
    norm_mix_g = 1.0 + 0.01 * nrm(ks[1], (L_, D_MODEL), f32)
    w_in = nrm(ks[2], (L_, D_MODEL, D_IN), f32) * D_MODEL ** -0.5
    s5_log_dt = jax.random.uniform(ks[3], (L_, S5_GROUPS), f32, math.log(1e-3), math.log(1e-1))
    s5_a_re = -0.5 + 0.01 * nrm(ks[4], (L_, S5_GROUPS, S5_STATE), f32)
    s5_a_im = jnp.pi * jnp.arange(S5_STATE, dtype=f32) + 0.01 * nrm(ks[5], (L_, S5_GROUPS, S5_STATE), f32)
    s5_b_re = nrm(ks[6], (L_, S5_GROUPS, S5_STATE, S5_GROUP), f32) * (2 * S5_GROUP) ** -0.5
    s5_b_im = nrm(ks[7], (L_, S5_GROUPS, S5_STATE, S5_GROUP), f32) * (2 * S5_GROUP) ** -0.5
    s5_c_re = nrm(ks[8], (L_, S5_GROUPS, S5_GROUP, S5_STATE), f32) * (2 * S5_STATE) ** -0.5
    s5_c_im = nrm(ks[9], (L_, S5_GROUPS, S5_GROUP, S5_STATE), f32) * (2 * S5_STATE) ** -0.5
    s5_d = nrm(ks[10], (L_, S5_WIDTH), f32)
    s5_w_glu = nrm(ks[11], (L_, S5_WIDTH, S5_WIDTH), f32) * S5_WIDTH ** -0.5
    s5_b_glu = 0.01 * nrm(ks[12], (L_, S5_WIDTH), f32)
    ml_conv_w = nrm(ks[13], (L_, CONV_WIDTH, 2 * ML_WIDTH), f32) * CONV_WIDTH ** -0.5
    ml_conv_b = 0.01 * nrm(ks[14], (L_, 2 * ML_WIDTH), f32)
    ml_b_gates = jnp.concatenate([
        0.1 * nrm(ks[15], (L_, ML_HEADS), f32),
        jnp.linspace(3.0, 6.0, ML_HEADS, dtype=f32) + 0.01 * nrm(ks[16], (L_, ML_HEADS), f32)], axis=-1)
    ml_norm_g = 1.0 + 0.01 * nrm(ks[17], (L_, ML_WIDTH), f32)
    w_out = nrm(ks[18], (L_, D_MIX, D_MODEL), f32) * D_MIX ** -0.5
    norm_ffn_g = 1.0 + 0.01 * nrm(ks[19], (L_, D_MODEL), f32)
    w_router = nrm(ks[20], (L_, D_MODEL, N_EXPERTS), f32) * D_MODEL ** -0.5
    b_router = 0.01 * nrm(ks[21], (L_, N_EXPERTS), f32)
    w_up = nrm(ks[22], (L_, N_EXPERTS, D_MODEL, 2 * D_FF), f32) * D_MODEL ** -0.5
    b_up = 0.01 * nrm(ks[23], (L_, N_EXPERTS, 2 * D_FF), f32)
    w_down = nrm(ks[24], (L_, N_EXPERTS, D_FF, D_MODEL), f32) * D_FF ** -0.5
    b_down = 0.01 * nrm(ks[25], (L_, N_EXPERTS, D_MODEL), f32)
    norm_final_g = 1.0 + 0.01 * nrm(ks[26], (D_MODEL,), f32)
    return {"x": x, "norm_mix_g": norm_mix_g, "w_in": w_in, "s5_log_dt": s5_log_dt,
            "s5_a_re": s5_a_re, "s5_a_im": s5_a_im, "s5_b_re": s5_b_re, "s5_b_im": s5_b_im,
            "s5_c_re": s5_c_re, "s5_c_im": s5_c_im, "s5_d": s5_d, "s5_w_glu": s5_w_glu,
            "s5_b_glu": s5_b_glu, "ml_conv_w": ml_conv_w, "ml_conv_b": ml_conv_b,
            "ml_b_gates": ml_b_gates, "ml_norm_g": ml_norm_g, "w_out": w_out,
            "norm_ffn_g": norm_ffn_g, "w_router": w_router, "b_router": b_router,
            "w_up": w_up, "b_up": b_up, "w_down": w_down, "b_down": b_down,
            "norm_final_g": norm_final_g}

def reference(x, norm_mix_g, w_in, s5_log_dt, s5_a_re, s5_a_im, s5_b_re, s5_b_im, s5_c_re,
              s5_c_im, s5_d, s5_w_glu, s5_b_glu, ml_conv_w, ml_conv_b, ml_b_gates, ml_norm_g,
              w_out, norm_ffn_g, w_router, b_router, w_up, b_up, w_down, b_down, norm_final_g):
    h = x
    o_q = S5_WIDTH
    o_k = o_q + ML_WIDTH
    o_v = o_k + ML_WIDTH
    o_o = o_v + ML_WIDTH
    o_g = o_o + ML_WIDTH
    for l in range(DEPTH):
        hn = rmsnorm(h, norm_mix_g[l])
        proj = hn @ w_in[l]
        y_s5 = s5_mixer(proj[..., :o_q], s5_log_dt[l], s5_a_re[l], s5_a_im[l], s5_b_re[l],
                        s5_b_im[l], s5_c_re[l], s5_c_im[l], s5_d[l], s5_w_glu[l], s5_b_glu[l])
        y_ml = mlstm_mixer(proj[..., o_q:o_k], proj[..., o_k:o_v], proj[..., o_v:o_o],
                           proj[..., o_o:o_g], proj[..., o_g:], ml_conv_w[l], ml_conv_b[l],
                           ml_b_gates[l], ml_norm_g[l])
        mix = jnp.concatenate([y_s5, y_ml], axis=-1)
        h = h + mix @ w_out[l]
        h = h + moe_ffn(rmsnorm(h, norm_ffn_g[l]), w_router[l], b_router[l], w_up[l], b_up[l],
                        w_down[l], b_down[l])
    return rmsnorm(h, norm_final_g)


_drawn_inputs = setup_inputs


def setup_inputs(seed=0):
    import zlib

    import numpy as np

    out = dict(_drawn_inputs(seed))
    spreads = {}
    factors = {'s5_a_re': 200.0,
     's5_b_glu': 28.436,
     'ml_conv_b': 4.111,
     'ml_norm_g': 8.963,
     'b_up': 8.0,
     'b_down': 49.867,
     'norm_final_g': 175.975,
     's5_log_dt': 25.583,
     's5_a_im': 30.528,
     's5_b_re': 37.624,
     's5_b_im': 36.792,
     's5_c_re': 28.264,
     's5_c_im': 37.704,
     'norm_ffn_g': 3.152,
     'b_router': 12.723}
    for name, (base, spread) in spreads.items():
        noise = np.random.default_rng([zlib.crc32(name.encode()), seed]).standard_normal(out[name].shape)
        drawn = base * np.exp(spread * noise) if base else spread * noise
        out[name] = __import__('jax').numpy.asarray(drawn.astype(out[name].dtype))
    for name, factor in factors.items():
        out[name] = (out[name] * factor).astype(out[name].dtype)
    return out
```

```python
from contextlib import ExitStack
import math

import concourse.bass as bass
from concourse import mybir

F32 = mybir.dt.float32
F32R = mybir.dt.float32r
BF16 = mybir.dt.bfloat16
U32 = mybir.dt.uint32
I32 = mybir.dt.int32
ALU = mybir.AluOpType
ACT = mybir.ActivationFunctionType
AX = mybir.AxisListType

P = 128
T = 1024
D = 1024
TT = T // P
KD = D // P
E = 32
K4 = 4
F = 1024
RMS_EPS = 1e-5
LN_EPS = 1e-6
LIMIT = 7.0
ALPHA = 1.702
BLOCKS = 3
SLOTS = BLOCKS * P
WAVES = -(-T // SLOTS)
CHUNKS = 12
RAW = 4
SPLIT = 3

HEADS, HD = 4, 128
MLW = HEADS * HD
S5W = 512
GROUPS, GP, GN = 32, 16, 64
SUB = 8
NCH = T // SUB
CH = 128
NC = T // CH
CONV = 4
CSTEPS = CONV + 1
PC = 256
PRAW = 2
GCOL = 64


def allocators(nc, ctx, prefix):
    def sb(name, shape, dt):
        return ctx.enter_context(nc.sbuf_tensor(prefix + name, shape, dt))

    def ps(name, shape, dt):
        return ctx.enter_context(nc.psum_tensor(prefix + name, shape, dt))

    sems = []

    def sem(name):
        sems.append(nc.alloc_semaphore(prefix + name))
        return sems[-1]

    def free():
        if sems:
            nc.clear_and_free_semaphores(sems)
            nc.all_engine_barrier()

    ctx.callback(free)

    return sb, ps, sem


def keep_tiles(nc, ctx):
    def sb(name, shape, dt):
        return ctx.enter_context(nc.sbuf_tensor("keep_" + name, shape, dt))

    return {
        "gates": sb("gates", [P, TT, K4], F32),
        "rank": sb("rank", [P, TT, E], F32),
        "picked": sb("picked", [P, TT, E, 3], BF16),
        "counts": sb("counts", [1, E], I32),
        "most": sb("most", [1, 1], I32),
        "more": sb("more", [1, (WAVES - 1) * E], I32),
        "order": sb("order", [1, (WAVES - 1) * E], I32),
        "slot_no": sb("slot_no", [P, WAVES * SLOTS], F32),
        "empty_at": sb("empty_at", [P, 1], F32),
        "row_pick": sb("row_pick", [2 * E, E], F32),
    }



def mixer_tiles(nc, ctx):
    def sb(name, shape, dt):
        return ctx.enter_context(nc.sbuf_tensor("mix_" + name, shape, dt))

    return {
        "qk": sb("qk", [P, 2 * HEADS, CONV - 1 + T], F32),
        "v": sb("v", [P, NC, HEADS, HD + 1], F32),
        "sig_o": sb("sig_o", [P, HEADS, T], F32),
        "gates": sb("gates", [HEADS, 2, T], F32),
    }




def project(nc, p, u_dram, mix):
    with ExitStack() as ctx:
        sb, ps, sem = allocators(nc, ctx, "pr_")
        x = sb("x", [P, 2, D], F32)
        gain = sb("gain", [P, D], F32)
        work = sb("work", [P, D], F32)
        sig = sb("sig", [P, D], F32)
        sumsq = sb("sumsq", [P, TT], F32)
        meansq = sb("meansq", [P, TT], F32)
        rstd = sb("rstd", [P, TT], F32)
        neg_half = sb("neg_half", [P, 1], F32)
        ident = sb("ident", [P, P], F32)
        h_hi = sb("h_hi", [P, KD, T], F32R)
        h_lo = sb("h_lo", [P, KD, T], F32R)
        raw = sb("raw", [P, PRAW, KD, PC], F32)
        w_hi = sb("w_hi", [P, 2, KD, PC], F32R)
        w_lo = sb("w_lo", [P, 2, KD, PC], F32R)
        conv_w = sb("conv_w", [P, CONV, 2 * HEADS], F32)
        conv_b = sb("conv_b", [P, 2 * HEADS], F32)
        b_gates = sb("b_gates", [HEADS, 2], F32)
        ps_t = [ps(f"ps_t{i}", [P, 512], F32) for i in range(2)]
        acc = [ps(f"acc{i}", [P, 512], F32) for i in range(4)]

        x_in = [sem(f"x_in{i}") for i in range(2)]
        gain_in = sem("gain_in")
        small_in = sem("small_in")
        f_gates_in = sem("f_gates_in")
        raw_full = [sem(f"raw_full{i}") for i in range(PRAW)]
        consts_set = sem("consts_set")
        squared = sem("squared")
        mean_set = sem("mean_set")
        rstd_set = sem("rstd_set")
        scaled = sem("scaled")
        turned = sem("turned")
        t_hi = sem("t_hi")
        t_free = sem("t_free")
        hi_done = sem("hi_done")
        lo_done = sem("lo_done")
        piece_used = sem("piece_used")
        unit_ready = sem("unit_ready")
        unit_read = sem("unit_read")
        conv_step = sem("conv_step")
        silu_sig = sem("silu_sig")
        u_out = [sem(f"u_out{i}") for i in range(2)]
        pads_set = sem("pads_set")

        q_at, v_at, o_at, g_at = S5W, S5W + 2 * MLW, S5W + 3 * MLW, S5W + 4 * MLW
        pieces = [("qk", q_at + i * PC, i) for i in range(2 * MLW // PC)]
        pieces += [("gates", g_at, 0)]
        pieces += [("u", i * PC, i) for i in range(S5W // PC)]
        pieces += [("v", v_at + i * PC, i) for i in range(MLW // PC)]
        pieces += [("o", o_at + i * PC, i) for i in range(MLW // PC)]
        TILES = PC // P
        units = []
        for n, (what, _, i) in enumerate(pieces):
            if what == "gates":
                units += [(n, what, 0, half) for half in range(2)]
            elif what == "v":
                units += [(n, what, i, pair) for pair in range(TT // 2)]
            else:
                units += [(n, what, TILES * i + c, half) for c in range(TILES) for half in range(2)]
        x_t = p["x"][0].rearrange("(j p) d -> p j d", p=P)
        w_in = p["w_in"][0].rearrange("(k p) n -> p k n", p=P)
        with nc.Block() as block:

            def load_piece(sp, n):
                what, at, _ = pieces[n]
                slot = n % PRAW
                if what == "gates":
                    src = w_in[:, :, at:at + 2 * HEADS].rearrange("p k (g h) -> p k g h", g=2)
                    sp.dma_start(raw[:, slot, :, 0:HEADS], src[:, :, 0, :]).then_inc(raw_full[slot], 16)
                    sp.dma_start(raw[:, slot, :, 32:32 + HEADS], src[:, :, 1, :]).then_inc(f_gates_in, 16)
                else:
                    sp.dma_start(raw[:, slot, :, :], w_in[:, :, at:at + PC]).then_inc(raw_full[slot], 16)

            @block.sync
            def _(sp):
                for j in range(TT):
                    if j >= 2:
                        sp.wait_ge(turned, 2 * (j - 1))
                    sp.dma_start(x[:, j % 2, :], x_t[:, j, :]).then_inc(x_in[j % 2], 16)
                    if j == 0:
                        sp.dma_start(gain[:, :], p["norm_mix_g"][0:1, :].to_broadcast([P, D])).then_inc(gain_in, 16)
                    if j < PRAW:
                        load_piece(sp, j)
                for n in range(PRAW, len(pieces)):
                    sp.wait_ge(lo_done, n - PRAW + 1)
                    load_piece(sp, n)

            @block.gpsimd
            def _(pool):
                with nc.allow_non_contiguous_dma(reason="small parameters, channels to partitions"):
                    pool.dma_start(conv_w[:, :, :], p["ml_conv_w"][0].rearrange("w (c p) -> p w c", p=P)).then_inc(small_in, 16)
                    pool.dma_start(conv_b[:, :], p["ml_conv_b"][0].rearrange("(c p) -> p c", p=P)).then_inc(small_in, 16)
                    pool.dma_start(b_gates[:, :], p["ml_b_gates"][0].rearrange("(g h) -> h g", h=HEADS)).then_inc(small_in, 16)
                pool.memset(neg_half[:, :], -0.5).then_inc(consts_set, 1)
                pool.memset(ident[:, :], 0.0).then_inc(consts_set, 1)
                pool.memset(mix["v"][:, :, :, :], 1.0).then_inc(consts_set, 1)
                for c in range(2 * HEADS):
                    pool.memset(mix["qk"][:, c, 0:CONV - 1], 0.0).then_inc(pads_set, 1)
                pool.wait_ge(consts_set, 3)
                pool.affine_select(out=ident[:, :], in_=ident[:, :], compare_op=ALU.not_equal, fill=1.0, base=0,
                                   pattern=[[-1, P]], channel_multiplier=1).then_inc(consts_set, 1)
                pool.wait_ge(consts_set, 4)
                for j in range(TT):
                    pool.wait_ge(mean_set, j + 1)
                    pool.tensor_tensor(rstd[:, j:j + 1], meansq[:, j:j + 1], neg_half[:, :], ALU.pow).then_inc(rstd_set, 1)
                for i in range(S5W // P):
                    pool.wait_ge(unit_read, units.index((*[n for n, u in enumerate(pieces) if u[0] == "u" and u[2] == i // TILES], "u", i, 1)) + 1)
                    pool.dma_start(u_dram[i * P:(i + 1) * P, :], x[:, i % 2, :]).then_inc(u_out[i % 2], 16)
                for i in range(2):
                    pool.wait_ge(u_out[i], 16 * (S5W // P) // 2)

            @block.scalar
            def _(act):
                def hi(n):
                    cols = GCOL if pieces[n][0] == "gates" else PC
                    act.wait_ge(raw_full[n % PRAW], 16 * (n // PRAW + 1))
                    if pieces[n][0] == "gates":
                        act.wait_ge(f_gates_in, 16)
                    if n >= 2:
                        act.wait_ge(piece_used, n - 1)
                    nc.scalar.copy(w_hi[:, n % 2, :, 0:cols], raw[:, n % PRAW, :, 0:cols]).then_inc(hi_done, 1)

                def square(j):
                    act.wait_ge(x_in[j % 2], 16 * (j // 2 + 1))
                    if j:
                        act.wait_ge(squared, j)
                    nc.scalar.activation(work[:, :], x[:, j % 2, :], ACT.Square, accum_out=sumsq[:, j:j + 1]).then_inc(squared, 1)

                square(0)
                for j in range(TT):
                    if j + 1 < TT:
                        square(j + 1)
                    for half in range(2):
                        act.wait_ge(turned, 2 * j + half + 1)
                        nc.scalar.copy(h_hi[:, 4 * half:4 * half + 4, j * P:(j + 1) * P],
                                       ps_t[half][:, :].rearrange("p (k t) -> p k t", k=4)).then_inc(t_hi, 1)
                    if j == 1:
                        hi(0)
                hi(1)
                silus = 0
                for m, (n, what, i, part) in enumerate(units):
                    if m and units[m - 1][0] != n and n + 1 < len(pieces):
                        hi(n + 1)
                    act.wait_ge(unit_ready, m + 1)
                    bank = acc[m % 4]
                    if what == "qk":
                        at = CONV - 1 + part * 512
                        nc.scalar.copy(mix["qk"][:, i, at:at + 512], bank[:, :]).then_inc(unit_read, 1)
                    elif what == "gates":
                        if part == 0:
                            act.wait_ge(small_in, 48)
                        for g in range(2):
                            ins = nc.scalar.activation(mix["gates"][:, g, part * 512:(part + 1) * 512],
                                                       bank[32 * g:32 * g + HEADS, :], ACT.Identity, bias=b_gates[:, g:g + 1])
                        ins.then_inc(unit_read, 1)
                    elif what == "u":
                        if i >= 2 and part == 0:
                            act.wait_ge(u_out[i % 2], 16 * (i // 2))
                        out = x[:, i % 2, :].rearrange("p (t c) -> p c t", t=SUB)[:, part * 64:(part + 1) * 64, :]
                        nc.scalar.copy(out, bank[:, :].rearrange("p (c t) -> p c t", t=SUB)).then_inc(unit_read, 1)
                    elif what == "v":
                        nc.scalar.copy(mix["v"][:, 2 * part:2 * part + 2, 2 * i:2 * i + 2, 0:HD],
                                       bank[:, :].rearrange("p (j h e) -> p j h e", j=2, h=2)).then_inc(unit_read, 1)
                    else:
                        nc.scalar.activation(mix["sig_o"][:, i, part * 512:(part + 1) * 512], bank[:, :],
                                             ACT.Sigmoid).then_inc(unit_read, 1)
                    if what in ("qk", "gates", "u") and silus < 2 * HEADS and m >= 2 * silus + 3:
                        act.wait_ge(conv_step, CSTEPS * silus + CONV)
                        nc.scalar.activation(sig[:, :], work[:, :], ACT.Sigmoid).then_inc(silu_sig, 1)
                        silus += 1
                assert silus == 2 * HEADS

            @block.tensor
            def _(pe):
                pe.wait_ge(consts_set, 4)
                for j in range(TT):
                    pe.wait_ge(scaled, j + 1)
                    for half in range(2):
                        if j:
                            pe.wait_ge(t_free, 2 * j + half - 1)
                        for k in range(4):
                            mm = pe.transpose(ps_t[half][:, k * P:(k + 1) * P],
                                              x[:, j % 2, (4 * half + k) * P:(4 * half + k + 1) * P], ident[:, :])
                        mm.then_inc(turned, 1)
                pe.wait_ge(t_free, 2 * TT)
                for m, (n, what, i, part) in enumerate(units):
                    if m == 0 or units[m - 1][0] != n:
                        pe.wait_ge(lo_done, n + 1)
                    if m >= 4:
                        pe.wait_ge(unit_read, m - 3)
                    s = n % 2
                    if what == "v":
                        for jj in range(2):
                            toks = slice((2 * part + jj) * P, (2 * part + jj + 1) * P)
                            to = acc[m % 4][:, jj * PC:(jj + 1) * PC]
                            for k in range(KD):
                                pe.matmul(to, h_hi[:, k, toks], w_hi[:, s, k, :], start=(k == 0), stop=False)
                                pe.matmul(to, h_hi[:, k, toks], w_lo[:, s, k, :], start=False, stop=False)
                                mm = pe.matmul(to, h_lo[:, k, toks], w_hi[:, s, k, :], start=False, stop=(k == KD - 1))
                    else:
                        cols = slice(0, GCOL) if what == "gates" else slice((i % TILES) * P, (i % TILES + 1) * P)
                        toks = slice(part * 512, (part + 1) * 512)
                        to = acc[m % 4][0:cols.stop - cols.start, :]
                        for k in range(KD):
                            pe.matmul(to, w_hi[:, s, k, cols], h_hi[:, k, toks], start=(k == 0), stop=False)
                            pe.matmul(to, w_hi[:, s, k, cols], h_lo[:, k, toks], start=False, stop=False)
                            mm = pe.matmul(to, w_lo[:, s, k, cols], h_hi[:, k, toks], start=False, stop=(k == KD - 1))
                    mm.then_inc(unit_ready, 1)
                    if m + 1 == len(units) or units[m + 1][0] != n:
                        pe.wait_ge(unit_ready, m + 1)
                        pe.sem_inc(piece_used, 1)

            @block.vector
            def _(v):
                def lo(n):
                    cols = GCOL if pieces[n][0] == "gates" else PC
                    v.wait_ge(hi_done, n + 1)
                    v.tensor_tensor(w_lo[:, n % 2, :, 0:cols], raw[:, n % PRAW, :, 0:cols],
                                    w_hi[:, n % 2, :, 0:cols].bitcast(F32), ALU.subtract).then_inc(lo_done, 1)

                def mean(j):
                    v.wait_ge(squared, j + 1)
                    v.tensor_scalar(meansq[:, j:j + 1], sumsq[:, j:j + 1], 1.0 / D, RMS_EPS, ALU.mult, ALU.add).then_inc(mean_set, 1)

                mean(0)
                v.wait_ge(gain_in, 16)
                for j in range(TT):
                    v.wait_ge(rstd_set, j + 1)
                    v.scalar_tensor_tensor(x[:, j % 2, :], x[:, j % 2, :], rstd[:, j:j + 1], gain[:, :],
                                           ALU.mult, ALU.mult).then_inc(scaled, 1)
                    if j + 1 < TT:
                        mean(j + 1)
                    for half in range(2):
                        v.wait_ge(t_hi, 2 * j + half + 1)
                        v.tensor_tensor(h_lo[:, 4 * half:4 * half + 4, j * P:(j + 1) * P],
                                        ps_t[half][:, :].rearrange("p (k t) -> p k t", k=4),
                                        h_hi[:, 4 * half:4 * half + 4, j * P:(j + 1) * P].bitcast(F32),
                                        ALU.subtract).then_inc(t_free, 1)
                    if j == 1:
                        lo(0)
                lo(1)
                v.wait_ge(small_in, 48)
                v.wait_ge(pads_set, 2 * HEADS)
                for c in range(2 * HEADS):
                    qk = mix["qk"][:, c, :]
                    v.wait_ge(unit_read, 2 * c + 2)
                    if c:
                        v.wait_ge(conv_step, CSTEPS * c)
                    v.tensor_scalar(work[:, :], qk[:, 0:T], conv_w[:, 0, c:c + 1], conv_b[:, c:c + 1], ALU.mult,
                                    ALU.add).then_inc(conv_step, 1)
                    for j in range(1, CONV):
                        v.wait_ge(conv_step, CSTEPS * c + j)
                        v.scalar_tensor_tensor(work[:, :], qk[:, j:j + T], conv_w[:, j, c:c + 1], work[:, :],
                                               ALU.mult, ALU.add).then_inc(conv_step, 1)
                    if c % 2 == 1 and c // 2 + 2 < len(pieces):
                        lo(c // 2 + 2)
                    v.wait_ge(silu_sig, c + 1)
                    v.scalar_tensor_tensor(qk[:, CONV - 1:], work[:, :], HD ** -0.5 if c < HEADS else 1.0, sig[:, :],
                                           ALU.mult, ALU.mult).then_inc(conv_step, 1)
                for n in range(HEADS + 2, len(pieces)):
                    lo(n)


def mlstm(nc, p, mix):
    with ExitStack() as ctx:
        sb, ps, sem = allocators(nc, ctx, "mlstm_")
        f_abs = sb("f_abs", [HEADS, T], F32)
        log_f = sb("log_f", [HEADS, T], F32)
        not_first = sb("not_first", [HEADS, T], F32)
        carry = sb("carry", [HEADS, T], F32)
        b = sb("b", [HEADS, T], F32)
        M = sb("M", [HEADS, T], F32)
        rows = sb("rows", [HEADS, 3, T], F32)
        ends = sb("ends", [HEADS, 2, NC], F32)
        sel = sb("sel", [HEADS, HEADS, P], F32)
        ident = sb("ident", [P, P], F32)
        mask = sb("mask", [P, P], F32)
        neg_half = sb("neg_half", [P, HEADS], F32)
        norm_g = sb("norm_g", [P, HEADS], F32)
        a_col = sb("a_col", [P, NC, HEADS], F32)
        w_state = sb("w_state", [P, NC, HEADS], F32)
        exp_neg_m = sb("exp_neg_m", [P, NC, HEADS], F32)
        m_before = sb("m_before", [P, HEADS, NC], F32)
        decay = sb("decay", [P, HEADS, NC], F32)
        masked = sb("masked", [P, HEADS, CH], F32)
        weight = sb("weight", [P, HEADS, CH], F32)
        w_inter = sb("w_inter", [P, HEADS, CH], F32)
        q_inter = sb("q_inter", [P, HEADS, CH], F32)
        intra = sb("intra", [P, HEADS, CH], F32)
        k_state = sb("k_state", [P, HEADS, HD], F32)
        C = sb("C", [P, 2, HEADS, HD + 1], F32)
        normed = sb("normed", [P, HEADS, HD], F32)
        denom = sb("denom", [P, HEADS], F32)
        inv = sb("inv", [P, HEADS], F32)
        stats = sb("stats", [P, HEADS, 6], F32)
        mean_var = sb("mean_var", [P, HEADS, 2], F32)
        var_h = sb("var_h", [P, HEADS], F32)
        rstd = sb("rstd", [P, HEADS], F32)
        scale = sb("scale", [P, HEADS], F32)
        shift = sb("shift", [P, HEADS], F32)
        ps_m = ps("ps_m", [P, 512], F32)
        ps_s = ps("ps_s", [P, 512], F32)
        ps_k = ps("ps_k", [P, 512], F32)
        ps_c = [ps(f"ps_c{i}", [P, 512], F32) for i in range(2)]
        ps_o = [ps(f"ps_o{i}", [P, 512], F32) for i in range(2)]
        ps_t = ps("ps_t", [P, 512], F32)

        small_in = sem("small_in")
        consts_set = sem("consts_set")
        abs_set, exp_set, log_set = sem("abs_set"), sem("exp_set"), sem("log_set")
        rows_set = sem("rows_set")
        cols_ready, cols_set = sem("cols_ready"), sem("cols_set")
        m_ready, m_read = sem("m_ready"), sem("m_read")
        mask_done, weight_done, inter_done = sem("mask_done"), sem("weight_done"), sem("inter_done")
        q_done = sem("q_done")
        s_ready, intra_done = sem("s_ready"), sem("intra_done")
        k_ready, k_done = sem("k_ready"), sem("k_done")
        c_ready, c_done = sem("c_ready"), sem("c_done")
        out_ready = sem("out_ready")
        var_done, pow_done = sem("var_done"), sem("pow_done")
        shift_done, normed_done = sem("shift_done"), sem("normed_done")
        t_ready, mix_done = sem("t_ready"), sem("mix_done")
        dve = sem("dve")

        q, k, v_aug = mix["qk"][:, 0:HEADS, CONV - 1:], mix["qk"][:, HEADS:, CONV - 1:], mix["v"]

        def steps(c):
            return slice(c * CH, (c + 1) * CH)

        def o_bank(h):
            return ps_o[h // 2][:, (h % 2) * (HD + 1):(h % 2 + 1) * (HD + 1)]

        def by_head(bank):
            return bank[:, :].rearrange("p (h t) -> p h t", h=HEADS)

        with nc.Block() as block:

            @block.sync
            def _(sp):
                with nc.allow_non_contiguous_dma(reason="small parameters, channels to partitions"):
                    sp.dma_start(norm_g[:, :], p["ml_norm_g"][0].rearrange("(h e) -> e h", e=HD)).then_inc(small_in, 16)

            @block.gpsimd
            def _(pool):
                pool.memset(ident[:, :], 0.0).then_inc(consts_set, 1)
                pool.memset(mask[:, :], 0.0).then_inc(consts_set, 1)
                pool.memset(sel[:, :, :], 0.0).then_inc(consts_set, 1)
                pool.memset(not_first[:, :], 1.0).then_inc(consts_set, 1)
                pool.memset(neg_half[:, :], -0.5).then_inc(consts_set, 1)
                pool.memset(ends[:, :, :], 0.0).then_inc(consts_set, 1)
                pool.memset(carry[:, :], 0.0).then_inc(consts_set, 1)
                pool.wait_ge(consts_set, 7)
                pool.affine_select(out=ident[:, :], in_=ident[:, :], compare_op=ALU.not_equal, fill=1.0, base=0,
                                   pattern=[[-1, P]], channel_multiplier=1).then_inc(consts_set, 1)
                pool.affine_select(out=mask[:, :], in_=mask[:, :], compare_op=ALU.is_ge, fill=-1e30, base=0,
                                   pattern=[[1, P]], channel_multiplier=-1).then_inc(consts_set, 1)
                pool.affine_select(out=sel[:, :, :], in_=sel[:, :, :], compare_op=ALU.not_equal, fill=1.0, base=0,
                                   pattern=[[-1, HEADS], [0, P]], channel_multiplier=1).then_inc(consts_set, 1)
                pool.memset(not_first[:, :].rearrange("h (c t) -> h c t", c=NC)[:, :, 0:1], 0.0).then_inc(consts_set, 1)
                for c in range(NC):
                    pool.wait_ge(inter_done, c + 1)
                    if c:
                        pool.wait_ge(out_ready, c)
                    pool.tensor_tensor(q_inter[:, :, :], q[:, :, steps(c)], w_inter[:, :, :], ALU.mult).then_inc(q_done, 1)
                    pool.wait_ge(var_done, c + 1)
                    pool.tensor_tensor(rstd[:, :], var_h[:, :], neg_half[:, :], ALU.pow).then_inc(pow_done, 1)

            @block.scalar
            def _(act):
                nc.scalar.activation(f_abs[:, :], mix["gates"][:, 1, :], ACT.Abs).then_inc(abs_set, 1)
                act.wait_ge(abs_set, 1)
                nc.scalar.activation(f_abs[:, :], f_abs[:, :], ACT.Exp, scale=-1.0).then_inc(exp_set, 1)
                act.wait_ge(exp_set, 1)
                nc.scalar.activation(f_abs[:, :], f_abs[:, :], ACT.Ln, bias=1.0).then_inc(log_set, 1)
                act.wait_ge(cols_ready, 1)
                nc.scalar.copy(a_col[:, :, :], ps_t[:, 0:32].rearrange("p (c h) -> p c h", c=NC)).then_inc(cols_set, 1)
                nc.scalar.activation(w_state[:, :, :], ps_t[:, 32:64].rearrange("p (c h) -> p c h", c=NC), ACT.Exp).then_inc(cols_set, 1)
                nc.scalar.activation(exp_neg_m[:, :, :], ps_t[:, 64:96].rearrange("p (c h) -> p c h", c=NC), ACT.Exp,
                                     scale=-1.0).then_inc(cols_set, 1)
                ends_b = ps_t[:, 96:160].rearrange("p (h r c) -> p h r c", h=HEADS, r=2)
                nc.scalar.copy(m_before[:, :, :], ends_b[:, :, 0, :]).then_inc(cols_set, 1)
                nc.scalar.activation(decay[:, :, :], ends_b[:, :, 1, :], ACT.Exp).then_inc(cols_set, 1)
                act.wait_ge(cols_set, 5)

                def weights(c):
                    act.wait_ge(mask_done, c + 1)
                    if c:
                        act.wait_ge(intra_done, c)
                    for h in range(HEADS):
                        ins = nc.scalar.activation(weight[:, h, :], masked[:, h, :], ACT.Exp, bias=a_col[:, c, h:h + 1])
                    ins.then_inc(weight_done, 1)
                    act.wait_ge(m_ready, c + 1)
                    if c:
                        act.wait_ge(q_done, c)
                    for h in range(HEADS):
                        ins = nc.scalar.activation(w_inter[:, h, :], by_head(ps_m)[:, h, :], ACT.Exp, scale=-1.0,
                                                   bias=m_before[:, h, c:c + 1])
                    ins.then_inc(inter_done, 1)

                weights(0)
                for c in range(NC):
                    if c + 1 < NC:
                        weights(c + 1)
                    act.wait_ge(shift_done, c + 1)
                    if c:
                        act.wait_ge(t_ready, c)
                    for h in range(HEADS):
                        ins = nc.scalar.activation(normed[:, h, :], o_bank(h)[:, 0:HD], ACT.Identity,
                                                   scale=scale[:, h:h + 1], bias=shift[:, h:h + 1])
                    ins.then_inc(normed_done, 1)

            @block.tensor
            def _(pe):
                pe.wait_ge(consts_set, 11)
                pe.wait_ge(rows_set, 1)
                for r in range(3):
                    for c in range(NC):
                        at = (r * NC + c) * HEADS
                        pe.transpose(ps_t[:, at:at + HEADS], rows[:, r, steps(c)], ident[0:HEADS, 0:HEADS])
                for h in range(HEADS):
                    mm = pe.matmul(ps_t[:, 96 + 16 * h:112 + 16 * h], sel[:, h, :],
                                   ends[:, :, :].rearrange("h r c -> h (r c)"), start=True, stop=True)
                mm.then_inc(cols_ready, 1)

                def spread_m(c):
                    if c:
                        pe.wait_ge(inter_done, c)
                        pe.wait_ge(mask_done, c)
                    for h in range(HEADS):
                        mm = pe.matmul(by_head(ps_m)[:, h, :], sel[:, h, :], M[:, steps(c)], start=True, stop=True)
                    mm.then_inc(m_ready, 1)

                def scores(c):
                    if c:
                        pe.wait_ge(intra_done, c)
                    for h in range(HEADS):
                        mm = pe.matmul(by_head(ps_s)[:, h, :], k[:, h, steps(c)], q[:, h, steps(c)], start=True, stop=True)
                    mm.then_inc(s_ready, 1)

                def turn_k(c):
                    if c:
                        pe.wait_ge(k_done, c)
                    for h in range(HEADS):
                        mm = pe.transpose(by_head(ps_k)[:, h, :], k[:, h, steps(c)], ident[:, :])
                    mm.then_inc(k_ready, 1)

                def turn_normed(c):
                    pe.wait_ge(normed_done, c + 1)
                    pe.wait_ge(mix_done, c) if c else pe.wait_ge(cols_set, 5)
                    for h in range(HEADS):
                        mm = pe.transpose(by_head(ps_t)[:, h, :], normed[:, h, :], ident[:, :])
                    mm.then_inc(t_ready, 1)

                spread_m(0)
                turn_k(0)
                scores(0)
                for c in range(NC):
                    if c + 1 < NC:
                        spread_m(c + 1)
                        pe.wait_ge(k_done, c + 1)
                        if c:
                            pe.wait_ge(c_done, c)
                        for h in range(HEADS):
                            to = ps_c[h // 2][:, (h % 2) * (HD + 1):(h % 2 + 1) * (HD + 1)]
                            mm = pe.matmul(to, k_state[:, h, :], v_aug[:, c, h, :], start=True, stop=True)
                        mm.then_inc(c_ready, 1)
                        turn_k(c + 1)
                    if c:
                        turn_normed(c - 1)
                    pe.wait_ge(intra_done, c + 1)
                    if c:
                        pe.wait_ge(q_done, c + 1)
                        pe.wait_ge(c_done, c)
                    for h in range(HEADS):
                        mm = pe.matmul(o_bank(h), intra[:, h, :], v_aug[:, c, h, :], start=True, stop=(c == 0))
                        if c:
                            mm = pe.matmul(o_bank(h), q_inter[:, h, :], C[:, c % 2, h, :], start=False, stop=True)
                    mm.then_inc(out_ready, 1)
                    if c + 1 < NC:
                        scores(c + 1)
                turn_normed(NC - 1)

            @block.vector
            def _(v):
                count = [0]

                def link(ins):
                    count[0] += 1
                    ins.then_inc(dve, 1)
                    v.wait_ge(dve, count[0])

                gate_i, gate_f = mix["gates"][:, 0, :], mix["gates"][:, 1, :]
                v.wait_ge(log_set, 1)
                link(v.scalar_tensor_tensor(log_f[:, :], gate_f, 0.0, f_abs[:, :], ALU.min, ALU.subtract))
                v.wait_ge(consts_set, 11)
                link(v.tensor_tensor_scan(b[:, :], not_first[:, :], log_f[:, :], 0.0, ALU.mult, ALU.add))
                link(v.tensor_tensor(rows[:, 0, :], gate_i, b[:, :], ALU.subtract))

                def by_chunk(row):
                    return row.rearrange("h (c t) -> h c t", c=NC)

                link(v.tensor_copy(by_chunk(carry[:, :])[:, 1:, 0], by_chunk(b[:, :])[:, :NC - 1, CH - 1]))
                link(v.tensor_tensor_scan(M[:, :], carry[:, :], rows[:, 0, :], 0.0, ALU.add, ALU.max))
                link(v.tensor_tensor(rows[:, 2, :], b[:, :], M[:, :], ALU.add))
                link(v.tensor_copy(ends[:, 0, 1:], by_chunk(rows[:, 2, :])[:, :NC - 1, CH - 1]))
                last = by_chunk(M[:, :])[:, :, CH - 1]
                link(v.tensor_tensor(ends[:, 1, :], ends[:, 0, :], last, ALU.subtract))
                v.tensor_tensor(by_chunk(rows[:, 1, :]), by_chunk(rows[:, 0, :]),
                                last.unsqueeze(2).to_broadcast([HEADS, NC, CH]), ALU.subtract).then_inc(rows_set, 1)

                def mask_m(c):
                    v.wait_ge(m_ready, c + 1)
                    if c:
                        v.wait_ge(weight_done, c)
                    v.tensor_tensor(masked[:, :, :], mask[:, :].unsqueeze(1).to_broadcast([P, HEADS, CH]),
                                    by_head(ps_m), ALU.subtract).then_inc(mask_done, 1)

                def gated(c):
                    v.wait_ge(t_ready, c + 1)
                    for h in range(HEADS):
                        o = mix["sig_o"][:, h, steps(c)]
                        ins = v.scalar_tensor_tensor(o, by_head(ps_t)[:, h, :], norm_g[:, h:h + 1], o, ALU.mult, ALU.mult)
                    ins.then_inc(mix_done, 1)

                mask_m(0)
                v.wait_ge(cols_set, 5)
                v.wait_ge(small_in, 16)
                for c in range(NC):
                    v.wait_ge(k_ready, c + 1)
                    if c:
                        v.wait_ge(c_ready, c)
                    v.tensor_tensor(k_state[:, :, :], by_head(ps_k),
                                    w_state[:, c, :].unsqueeze(2).to_broadcast([P, HEADS, HD]), ALU.mult).then_inc(k_done, 1)
                    v.wait_ge(s_ready, c + 1)
                    v.wait_ge(weight_done, c + 1)
                    if c:
                        v.wait_ge(out_ready, c)
                    v.tensor_tensor(intra[:, :, :], by_head(ps_s), weight[:, :, :], ALU.mult).then_inc(intra_done, 1)
                    if c + 1 < NC:
                        mask_m(c + 1)
                        v.wait_ge(c_ready, c + 1)
                        if c:
                            v.wait_ge(c_done, c)
                        for h in range(HEADS):
                            new = ps_c[h // 2][:, (h % 2) * (HD + 1):(h % 2 + 1) * (HD + 1)]
                            if c == 0:
                                ins = v.tensor_copy(C[:, 1, h, :], new)
                            else:
                                ins = v.scalar_tensor_tensor(C[:, (c + 1) % 2, h, :], C[:, c % 2, h, :],
                                                             decay[:, h, c:c + 1], new, ALU.mult, ALU.add)
                        ins.then_inc(c_done, 1)
                    if c:
                        gated(c - 1)
                    v.wait_ge(out_ready, c + 1)
                    den = [ps_o[i][:, 0:2 * (HD + 1)].rearrange("p (h e) -> p h e", h=2)[:, :, HD] for i in range(2)]
                    for i in range(2):
                        ins = v.scalar_tensor_tensor(denom[:, 2 * i:2 * i + 2], den[i], -1.0,
                                                     exp_neg_m[:, c, 2 * i:2 * i + 2], ALU.mult, ALU.max)
                    link(ins)
                    for i in range(2):
                        ins = v.tensor_tensor(denom[:, 2 * i:2 * i + 2], den[i], denom[:, 2 * i:2 * i + 2], ALU.max)
                    link(ins)
                    for h in range(HEADS):
                        ins = v.bn_stats(stats[:, h, :], o_bank(h)[:, 0:HD])
                    link(ins)
                    v.reciprocal(inv[:, :], denom[:, :])
                    for h in range(HEADS):
                        ins = v.bn_aggr(mean_var[:, h, :], stats[:, h, :])
                    link(ins)
                    link(v.tensor_tensor(var_h[:, :], mean_var[:, :, 1], inv[:, :], ALU.mult))
                    link(v.tensor_tensor(var_h[:, :], var_h[:, :], inv[:, :], ALU.mult))
                    v.tensor_scalar(var_h[:, :], var_h[:, :], LN_EPS, None, ALU.add).then_inc(var_done, 1)
                    v.wait_ge(pow_done, c + 1)
                    if c:
                        v.wait_ge(normed_done, c)
                    link(v.tensor_tensor(scale[:, :], rstd[:, :], inv[:, :], ALU.mult))
                    v.scalar_tensor_tensor(shift[:, :], mean_var[:, :, 0], -1.0, scale[:, :], ALU.mult, ALU.mult).then_inc(shift_done, 1)
                gated(NC - 1)


def s5(nc, p, u_dram, g_dram, mix):
    with ExitStack() as ctx:
        sb, ps, sem = allocators(nc, ctx, "s5x_")
        HG = GROUPS // 2
        Q = 4
        QUADS = HG // Q
        U = sb("U", [P, GROUPS, NCH], F32)
        in1 = sb("in1", [P, GROUPS, GP], F32)
        in2 = sb("in2", [P, GROUPS, GP], F32)
        Bbar = sb("Bbar", [P, GROUPS, GP], F32)
        Bswap = sb("Bswap", [P, GROUPS, GP], F32)
        Cc = sb("Cc", [P, GROUPS, GP], F32)
        Cs = sb("Cs", [P, GROUPS, GP], F32)
        a_rows = sb("a_rows", [GROUPS, 2, P], F32)
        ident = sb("ident", [P, P], F32)
        sgn = sb("sgn", [P, 1], F32)
        neg_sgn = sb("neg_sgn", [P, 1], F32)
        skip_d = sb("skip_d", [P, GROUPS], F32)
        small = {n: sb(n, [P, GROUPS], F32) for n in
                 ("a_re", "a_im", "dt", "mag", "theta", "turns", "cos1", "sin1", "t0", "t1", "t2", "t3",
                  "coef_re", "coef_im", "rho1", "cos8", "sin8")}
        pow_re = sb("pow_re", [P, GROUPS, SUB + 1], F32)
        pow_im = sb("pow_im", [P, GROUPS, SUB + 1], F32)
        rev_re = sb("rev_re", [P, GROUPS, SUB], F32)
        rev_im = sb("rev_im", [P, GROUPS, SUB], F32)
        pw = [sb(f"pw{i}", [P, GROUPS, SUB // 2], F32) for i in range(2)]
        E_pad = sb("E_pad", [P, HG, 2 * SUB - 1, GP], F32)
        W = sb("W", [P, HG, P], F32)
        W_back = sb("W_back", [P, HG, P], F32)
        toep = sb("toep", [P, HG, P], F32)
        V = sb("V", [P, HG, SUB, GP], F32)
        V_back = sb("V_back", [P, HG, SUB, GP], F32)
        cos = sb("cos", [P, HG, NCH], F32)
        sin = sb("sin", [P, HG, NCH], F32)
        rho = sb("rho", [P, HG, NCH], F32)
        Z = sb("Z", [P, HG, NCH], F32)
        skip = sb("skip", [P, HG, NCH], F32)
        c_rows = skip[:, 0:8, :].rearrange("p (w j) n -> p w j n", w=2)
        spare = mix["v"][:, :, :, :].rearrange("p c h e -> p (c h e)")
        tmp1 = spare[:, 0:HG * NCH].rearrange("p (g c) -> p g c", g=HG)
        tmp2 = spare[:, HG * NCH:2 * HG * NCH].rearrange("p (g c) -> p g c", g=HG)
        ps_w = [ps(f"ps_w{i}", [P, 512], F32) for i in range(2)]
        ps_k = [ps(f"ps_k{i}", [P, 512], F32) for i in range(2)]
        ps_s = ps("ps_s", [P, 512], F32)
        ps_b = ps("ps_b", [P, 512], F32)
        ps_y = [ps(f"ps_y{i}", [P, 512], F32) for i in range(2)]

        u_in = sem("u_in")

        def by4(bank):
            return bank[:, :].rearrange("p (g c) -> p g c", g=Q)

        with ExitStack() as ctx2:
            _, _, sem = allocators(nc, ctx2, "s5t_")
            params_in, b_in, c_in, d_in = sem("params_in"), sem("b_in"), sem("c_in"), sem("d_in")
            consts_set = sem("consts_set")
            dt_set, turned, dve, act_done, rev_done = (sem("dt_set"), sem("turned"), sem("dve"), sem("act_done"),
                                                       sem("rev_done"))
            s = small
            TURN = 2 * math.pi
            TURN1 = 6.28125
            TURN2 = 1.934528350830078e-03
            TURN3 = TURN - TURN1 - TURN2
            with nc.Block() as block:

                @block.sync
                def _(sp):
                    for half in range(2):
                        cols = slice(GN * half, GN * (half + 1))
                        sp.dma_start(a_rows[:, 0, cols], p["s5_a_re"][0]).then_inc(params_in, 16)
                        sp.dma_start(a_rows[:, 1, cols], p["s5_a_im"][0]).then_inc(params_in, 16)
                    sp.dma_start(s["dt"][:, :], p["s5_log_dt"][0:1, :].to_broadcast([P, GROUPS])).then_inc(params_in, 16)
                    for which in range(2):
                        names = ("s5_c_re", "s5_c_im") if which == 0 else ("s5_c_im", "s5_c_re")
                        for half in range(2):
                            sp.dma_start(c_rows[:, which, :, GN * half:GN * (half + 1)],
                                         p[names[half]][0].rearrange("(j g) p n -> (g p) j n", j=4)).then_inc(c_in, 16)
                    with nc.allow_non_contiguous_dma(reason="64-byte runs"):
                        for which, tile in enumerate((in1, in2)):
                            names = ("s5_b_re", "s5_b_im") if which == 0 else ("s5_b_im", "s5_b_re")
                            for half in range(2):
                                sp.dma_start(tile[GN * half:GN * (half + 1), :, :],
                                             p[names[half]][0].rearrange("g n p -> n g p")).then_inc(b_in, 16)
                    for t in range(SUB):
                        sp.dma_start(U[GP * t:GP * (t + 1), :, :],
                                     u_dram[:, t * NCH:(t + 1) * NCH].rearrange("(g p) c -> p g c", p=GP)).then_inc(u_in, 16)
                    with nc.allow_non_contiguous_dma(reason="small parameters, channels to partitions"):
                        for t in range(SUB):
                            sp.dma_start(skip_d[GP * t:GP * (t + 1), :],
                                         p["s5_d"][0].rearrange("(g p) -> p g", p=GP)).then_inc(d_in, 16)
                    sp.wait_ge(u_in, 16 * SUB)
                    sp.wait_ge(d_in, 16 * SUB)

                @block.gpsimd
                def _(pool):
                    pool.memset(ident[:, :], 0.0).then_inc(consts_set, 1)
                    for n, (tile, rows, value) in enumerate(((sgn, slice(0, GN), -1.0), (sgn, slice(GN, P), 1.0),
                                                             (neg_sgn, slice(0, GN), 1.0), (neg_sgn, slice(GN, P), -1.0))):
                        pool.wait_ge(consts_set, n + 1)
                        pool.memset(tile[rows, :], value).then_inc(consts_set, 1)
                    pool.wait_ge(consts_set, 5)
                    pool.memset(pow_re[:, :, 0], 1.0).then_inc(consts_set, 1)
                    pool.memset(pow_im[:, :, 0], 0.0).then_inc(consts_set, 1)
                    pool.memset(E_pad[:, :, SUB:, :], 0.0).then_inc(consts_set, 1)
                    pool.wait_ge(consts_set, 8)
                    pool.affine_select(out=ident[:, :], in_=ident[:, :], compare_op=ALU.not_equal, fill=1.0, base=0,
                                       pattern=[[-1, P]], channel_multiplier=1).then_inc(consts_set, 1)

                @block.tensor
                def _(pe):
                    pe.wait_ge(consts_set, 9)
                    pe.wait_ge(params_in, 80)
                    pe.wait_ge(c_in, 64)
                    for r in range(2):
                        mm = pe.transpose(ps_s[:, r * GROUPS:(r + 1) * GROUPS], a_rows[:, r, :], ident[0:GROUPS, 0:GROUPS])
                    for which in range(2):
                        for j in range(4):
                            mm = pe.transpose(ps_w[which][:, j * P:(j + 1) * P], c_rows[:, which, j, :], ident[:, :])
                    mm.then_inc(turned, 1)

                @block.scalar
                def _(act):
                    act.wait_ge(params_in, 80)
                    nc.scalar.activation(s["dt"][:, :], s["dt"][:, :], ACT.Exp).then_inc(dt_set, 1)
                    act.wait_ge(rev_done, 1)
                    nc.scalar.activation(s["mag"][:, :], s["t0"][:, :], ACT.Exp).then_inc(act_done, 1)
                    act.wait_ge(rev_done, 2)
                    nc.scalar.activation(s["sin1"][:, :], s["theta"][:, :], ACT.Sin).then_inc(act_done, 1)
                    nc.scalar.activation(s["cos1"][:, :], s["turns"][:, :], ACT.Sin).then_inc(act_done, 1)

                @block.vector
                def _(v):
                    count = [0]

                    def link(ins):
                        count[0] += 1
                        ins.then_inc(dve, 1)
                        v.wait_ge(dve, count[0])

                    def product(re, im, x_re, x_im, y_re, y_im, t0, t1):
                        link(v.tensor_tensor(re, x_re, y_re, ALU.mult))
                        link(v.tensor_tensor(t0, x_im, y_im, ALU.mult))
                        link(v.tensor_tensor(re, re, t0, ALU.subtract))
                        link(v.tensor_tensor(im, x_re, y_im, ALU.mult))
                        link(v.tensor_tensor(t1, x_im, y_re, ALU.mult))
                        link(v.tensor_tensor(im, im, t1, ALU.add))

                    t0, t1, t2, t3 = (s[n][:, :] for n in ("t0", "t1", "t2", "t3"))
                    a_re, a_im, dt, theta, turns = (s[n][:, :] for n in ("a_re", "a_im", "dt", "theta", "turns"))
                    v.wait_ge(turned, 1)
                    link(v.tensor_scalar(a_re, ps_s[:, 0:GROUPS], -1e-4, None, ALU.min))
                    link(v.tensor_copy(a_im, ps_s[:, GROUPS:2 * GROUPS]))
                    v.wait_ge(dt_set, 1)
                    v.tensor_tensor(t0, dt, a_re, ALU.mult).then_inc(rev_done, 1)
                    link(v.tensor_tensor(theta, dt, a_im, ALU.mult))
                    link(v.tensor_scalar(turns, theta, 1.0 / TURN, None, ALU.mult))
                    link(v.tensor_scalar(turns, turns, 12582912.0, None, ALU.add))
                    link(v.tensor_scalar(turns, turns, -12582912.0, None, ALU.add))
                    for part in (TURN1, TURN2, TURN3):
                        link(v.scalar_tensor_tensor(theta, turns, -part, theta, ALU.mult, ALU.add))
                    link(v.tensor_scalar(theta, theta, 3.1415925, -3.1415925, ALU.min, ALU.max))
                    link(v.scalar_tensor_tensor(turns, theta, -1.0, theta, ALU.mult, ALU.min))
                    v.tensor_scalar(turns, turns, math.pi / 2, None, ALU.add).then_inc(rev_done, 1)
                    v.wait_ge(consts_set, 9)
                    v.tensor_scalar(Cc[:, :, :].rearrange("p g q -> p (g q)"), ps_w[0][:, :], neg_sgn[:, 0:1], None, ALU.mult)
                    link(v.tensor_copy(Cs[:, :, :].rearrange("p g q -> p (g q)"), ps_w[1][:, :]))
                    v.wait_ge(act_done, 3)
                    mag, cos1, sin1 = s["mag"][:, :], s["cos1"][:, :], s["sin1"][:, :]
                    link(v.tensor_tensor(pow_re[:, :, 1], mag, cos1, ALU.mult))
                    link(v.tensor_tensor(pow_im[:, :, 1], mag, sin1, ALU.mult))
                    link(v.tensor_tensor(t1, a_re, a_re, ALU.mult))
                    link(v.tensor_tensor(t2, a_im, a_im, ALU.mult))
                    link(v.tensor_tensor(t1, t1, t2, ALU.add))
                    link(v.reciprocal(t1, t1))
                    link(v.tensor_scalar(t0, pow_re[:, :, 1], -1.0, None, ALU.add))
                    link(v.tensor_tensor(t2, t0, a_re, ALU.mult))
                    link(v.tensor_tensor(t3, pow_im[:, :, 1], a_im, ALU.mult))
                    link(v.tensor_tensor(t2, t2, t3, ALU.add))
                    link(v.tensor_tensor(s["coef_re"][:, :], t2, t1, ALU.mult))
                    link(v.tensor_tensor(t2, pow_im[:, :, 1], a_re, ALU.mult))
                    link(v.tensor_tensor(t3, t0, a_im, ALU.mult))
                    link(v.tensor_tensor(t2, t2, t3, ALU.subtract))
                    link(v.scalar_tensor_tensor(s["coef_im"][:, :], t2, sgn[:, 0:1], t1, ALU.mult, ALU.mult))
                    v.wait_ge(b_in, 64)
                    c_re = s["coef_re"][:, :].unsqueeze(2).to_broadcast([P, GROUPS, GP])
                    c_im = s["coef_im"][:, :].unsqueeze(2).to_broadcast([P, GROUPS, GP])
                    link(v.tensor_tensor(Bbar[:, :, :], in1[:, :, :], c_re, ALU.mult))
                    link(v.tensor_tensor(Bswap[:, :, :], in2[:, :, :], c_re, ALU.mult))
                    link(v.tensor_tensor(in2[:, :, :], in2[:, :, :], c_im, ALU.mult))
                    link(v.tensor_tensor(in1[:, :, :], in1[:, :, :], c_im, ALU.mult))
                    link(v.tensor_tensor(Bbar[:, :, :], Bbar[:, :, :], in2[:, :, :], ALU.add))
                    link(v.tensor_tensor(Bswap[:, :, :], Bswap[:, :, :], in1[:, :, :], ALU.subtract))
                    n = 1
                    while n < SUB:
                        def spread(tile):
                            return tile[:, :, n:n + 1].to_broadcast([P, GROUPS, n])
                        product(pow_re[:, :, n + 1:2 * n + 1], pow_im[:, :, n + 1:2 * n + 1],
                                pow_re[:, :, 1:n + 1], pow_im[:, :, 1:n + 1], spread(pow_re), spread(pow_im),
                                pw[0][:, :, 0:n], pw[1][:, :, 0:n])
                        n *= 2
                    for k in range(SUB):
                        v.tensor_copy(rev_re[:, :, k], pow_re[:, :, SUB - 1 - k])
                        link(v.tensor_scalar(rev_im[:, :, k], pow_im[:, :, SUB - 1 - k], sgn[:, 0:1], None, ALU.mult))
                    link(v.tensor_tensor(s["rho1"][:, :], mag, mag, ALU.mult))
                    link(v.tensor_tensor(s["rho1"][:, :], s["rho1"][:, :], s["rho1"][:, :], ALU.mult))
                    link(v.tensor_tensor(s["rho1"][:, :], s["rho1"][:, :], s["rho1"][:, :], ALU.mult))
                    product(s["cos8"][:, :], s["sin8"][:, :], cos1, sin1, cos1, sin1, t0, t1)
                    product(t2, t3, s["cos8"][:, :], s["sin8"][:, :], s["cos8"][:, :], s["sin8"][:, :], t0, t1)
                    product(s["cos8"][:, :], s["sin8"][:, :], t2, t3, t2, t3, t0, t1)

        for half in range(2):
            G = slice(half * HG, (half + 1) * HG)
            with ExitStack() as ctx2:
                _, _, sem = allocators(nc, ctx2, f"s5h{half}_")
                e_parts, e_done = sem("e_parts"), sem("e_done")
                pool_seq, dve = sem("pool_seq"), sem("dve")
                w_ready, w_done = sem("w_ready"), sem("w_done")
                k_ready, k_done = sem("k_ready"), sem("k_done")
                s_ready, s_read = sem("s_ready"), sem("s_read")
                z_done, y_ready, y_read = sem("z_done"), sem("y_ready"), sem("y_read")
                cube_done, sig_done, g_done, g_out = sem("cube_done"), sem("sig_done"), sem("g_done"), sem("g_out")
                skip_done = sem("skip_done")
                v_back_done = sem("v_back_done")
                shape = [P, HG, SUB, GP]

                def over_steps(x):
                    return x[:, G, :].unsqueeze(2).to_broadcast(shape)

                def over_channels(x):
                    return x.unsqueeze(3).to_broadcast(shape)

                def as4(x):
                    return x.rearrange("p g (s q) -> p g s q", s=SUB)

                with nc.Block() as block:

                    @block.sync
                    def _(sp):
                        for quad in range(QUADS):
                            sp.wait_ge(g_done, quad + 1)
                        for t in range(SUB):
                            sp.dma_start(g_dram[:, t * NCH:(t + 1) * NCH].rearrange("(g p) c -> p g c", p=GP)[:, G, :],
                                         Z[GP * t:GP * (t + 1), :, :]).then_inc(g_out, 16)
                        sp.wait_ge(g_out, 16 * SUB)

                    @block.gpsimd
                    def _(pool):
                        count = [0]

                        def link(ins):
                            count[0] += 1
                            ins.then_inc(pool_seq, 1)
                            pool.wait_ge(pool_seq, count[0])

                        pool.tensor_tensor(as4(tmp2), over_steps(Bswap), over_channels(rev_im[:, G, :]), ALU.mult).then_inc(e_parts, 1)
                        link(pool.tensor_copy(rho[:, :, :], small["rho1"][:, G].unsqueeze(2).to_broadcast([P, HG, NCH])))
                        link(pool.memset(rho[:, :, 0:1], 0.0))
                        link(pool.tensor_tensor(V_back[:, :, :, :], over_steps(Cs), over_channels(pow_re[:, G, 1:]), ALU.mult))
                        link(pool.tensor_tensor(as4(skip[:, :, :]), over_steps(Cc), over_channels(pow_im[:, G, 1:]), ALU.mult))
                        link(pool.tensor_tensor(V_back[:, :, :, :], V_back[:, :, :, :], as4(skip[:, :, :]), ALU.add))
                        pool.tensor_tensor(skip[:, :, :], U[:, G, :], skip_d[:, G].unsqueeze(2).to_broadcast([P, HG, NCH]),
                                           ALU.mult).then_inc(skip_done, 1)

                    @block.scalar
                    def _(act):
                        for quad in range(QUADS):
                            g = slice(quad * Q, (quad + 1) * Q)
                            act.wait_ge(w_ready, quad + 1)
                            bank = by4(ps_w[quad % 2])
                            nc.scalar.copy(W[:, g, :], bank)
                            nc.scalar.copy(W_back[:, g, 0:GN], bank[:, :, GN:])
                            nc.scalar.mul(W_back[:, g, GN:], bank[:, :, 0:GN], -1.0).then_inc(w_done, 1)
                            act.wait_ge(k_ready, quad + 1)
                            nc.scalar.copy(toep[:, g, :], by4(ps_k[quad % 2])).then_inc(k_done, 1)
                        for quad in range(QUADS):
                            g = slice(quad * Q, (quad + 1) * Q)
                            act.wait_ge(cube_done, quad + 1)
                            nc.scalar.activation(skip[:, g, :], skip[:, g, :], ACT.Sigmoid, scale=2 * math.sqrt(2 / math.pi)).then_inc(sig_done, 1)

                    @block.tensor
                    def _(pe):
                        pe.wait_ge(e_done, 1)
                        for quad in range(QUADS):
                            if quad >= 2:
                                pe.wait_ge(w_done, quad - 1)
                            for i in range(Q):
                                mm = pe.transpose(by4(ps_w[quad % 2])[:, i, :],
                                                  E_pad[:, quad * Q + i, 0:SUB, :].rearrange("p s q -> p (s q)"), ident[:, :])
                            mm.then_inc(w_ready, 1)
                            if quad >= 2:
                                pe.wait_ge(k_done, quad - 1)
                            for i in range(Q):
                                for t in range(SUB):
                                    at = i * P + t * GP
                                    mm = pe.matmul(ps_k[quad % 2][:, at:at + GP],
                                                   E_pad[:, quad * Q + i, SUB - 1 - t:2 * SUB - 1 - t, :].rearrange("p s q -> p (s q)"),
                                                   Cc[:, half * HG + quad * Q + i, :], start=True, stop=True)
                            mm.then_inc(k_ready, 1)
                        for quad in range(QUADS):
                            pe.wait_ge(w_done, quad + 1)
                            if quad:
                                pe.wait_ge(s_read, quad)
                            for bank, w in ((ps_s, W), (ps_b, W_back)):
                                for i in range(Q):
                                    n = quad * Q + i
                                    mm = pe.matmul(by4(bank)[:, i, :], w[:, n, :], U[:, half * HG + n, :], start=True, stop=True)
                            mm.then_inc(s_ready, 1)
                        pe.wait_ge(v_back_done, 1)
                        pe.wait_ge(skip_done, 1)
                        for quad in range(QUADS):
                            pe.wait_ge(z_done, quad + 1)
                            pe.wait_ge(k_done, quad + 1)
                            if quad >= 2:
                                pe.wait_ge(y_read, quad - 1)
                            for i in range(Q):
                                n = quad * Q + i
                                to = by4(ps_y[quad % 2])[:, i, :]
                                pe.matmul(to, toep[:, n, :], U[:, half * HG + n, :], start=True, stop=False)
                                pe.matmul(to[:, 1:], V[:, n, :, :].rearrange("p s q -> p (s q)"), tmp1[:, n, 0:NCH - 1],
                                          start=False, stop=False)
                                mm = pe.matmul(to[:, 1:], V_back[:, n, :, :].rearrange("p s q -> p (s q)"),
                                               tmp2[:, n, 0:NCH - 1], start=False, stop=True)
                            mm.then_inc(y_ready, 1)

                    @block.vector
                    def _(v):
                        count = [0]

                        def link(ins):
                            count[0] += 1
                            ins.then_inc(dve, 1)
                            v.wait_ge(dve, count[0])

                        link(v.tensor_tensor(as4(tmp1), over_steps(Bbar), over_channels(rev_re[:, G, :]), ALU.mult))
                        v.wait_ge(e_parts, 1)
                        v.tensor_tensor(E_pad[:, :, 0:SUB, :], as4(tmp1), as4(tmp2), ALU.add).then_inc(e_done, 1)
                        v.wait_ge(e_done, 1)
                        link(v.tensor_copy(cos[:, :, 0], small["cos8"][:, G]))
                        link(v.tensor_copy(sin[:, :, 0], small["sin8"][:, G]))
                        n = 1
                        while n < NCH:
                            done, new = slice(0, n), slice(n, 2 * n)

                            def last(x):
                                return x[:, :, n - 1:n].to_broadcast([P, HG, n])
                            v.tensor_tensor(tmp1[:, :, new], cos[:, :, done], last(cos), ALU.mult)
                            link(v.tensor_tensor(tmp2[:, :, new], sin[:, :, done], last(sin), ALU.mult))
                            link(v.tensor_tensor(cos[:, :, new], tmp1[:, :, new], tmp2[:, :, new], ALU.subtract))
                            v.tensor_tensor(tmp1[:, :, new], cos[:, :, done], last(sin), ALU.mult)
                            link(v.tensor_tensor(tmp2[:, :, new], sin[:, :, done], last(cos), ALU.mult))
                            link(v.tensor_tensor(sin[:, :, new], tmp1[:, :, new], tmp2[:, :, new], ALU.add))
                            n *= 2
                        link(v.tensor_tensor(V[:, :, :, :], over_steps(Cc), over_channels(pow_re[:, G, 1:]), ALU.mult))
                        link(v.tensor_tensor(as4(Z[:, :, :]), over_steps(Cs), over_channels(pow_im[:, G, 1:]), ALU.mult))
                        link(v.tensor_tensor(V[:, :, :, :], V[:, :, :, :], as4(Z[:, :, :]), ALU.subtract))
                        v.wait_ge(pool_seq, 5)
                        v.sem_inc(v_back_done, 1)

                        def flat(x, g):
                            return x[:, g, :].rearrange("p g c -> p (g c)")
                        for quad in range(QUADS):
                            g = slice(quad * Q, (quad + 1) * Q)
                            v.wait_ge(s_ready, quad + 1)
                            v.tensor_tensor(tmp1[:, g, :], by4(ps_s), cos[:, g, :], ALU.mult)
                            link(v.tensor_tensor(tmp2[:, g, :], by4(ps_b), sin[:, g, :], ALU.mult))
                            v.tensor_tensor(tmp1[:, g, :], tmp1[:, g, :], tmp2[:, g, :], ALU.add).then_inc(s_read, 1)
                            v.wait_ge(s_read, quad + 1)
                            link(v.tensor_tensor_scan(flat(Z, g), flat(rho, g), flat(tmp1, g), 0.0, ALU.mult, ALU.add))
                            v.tensor_tensor(tmp1[:, g, :], Z[:, g, :], cos[:, g, :], ALU.mult)
                            v.scalar_tensor_tensor(tmp2[:, g, :], Z[:, g, :], -1.0, sin[:, g, :], ALU.mult, ALU.mult).then_inc(z_done, 1)
                        v.wait_ge(skip_done, 1)
                        for quad in range(QUADS):
                            g = slice(quad * Q, (quad + 1) * Q)
                            y = Z[:, g, :]
                            v.wait_ge(y_ready, quad + 1)
                            v.wait_ge(z_done, quad + 1)
                            v.tensor_tensor(y, skip[:, g, :], by4(ps_y[quad % 2]), ALU.add).then_inc(y_read, 1)
                            v.wait_ge(y_read, quad + 1)
                            link(v.tensor_tensor(skip[:, g, :], y, y, ALU.mult))
                            link(v.tensor_scalar(skip[:, g, :], skip[:, g, :], 0.044715, 1.0, ALU.mult, ALU.add))
                            v.tensor_tensor(skip[:, g, :], skip[:, g, :], y, ALU.mult).then_inc(cube_done, 1)
                        for quad in range(QUADS):
                            g = slice(quad * Q, (quad + 1) * Q)
                            v.wait_ge(sig_done, quad + 1)
                            v.tensor_tensor(Z[:, g, :], Z[:, g, :], skip[:, g, :], ALU.mult).then_inc(g_done, 1)

    with ExitStack() as ctx:
        sb, ps, sem = allocators(nc, ctx, "s5g_")
        KG = S5W // P
        g = sb("g", [P, KG, T], F32)
        w = sb("w", [P, KG, S5W], F32)
        b = sb("b", [P, KG], F32)
        gate = sb("gate", [P, 2, 512], F32)
        acc = [ps(f"acc{i}", [P, 512], F32) for i in range(4)]
        g_in, w_in, b_in = sem("g_in"), sem("w_in"), sem("b_in")
        ready, gate_done, out_done = sem("ready"), sem("gate_done"), sem("out_done")
        units = [(i, half) for i in range(KG) for half in range(2)]
        with nc.Block() as block:

            @block.sync
            def _(sp):
                sp.dma_start(w[:, :, :], p["s5_w_glu"][0].rearrange("(k p) n -> p k n", p=P)).then_inc(w_in, 16)
                sp.dma_start(g[:, :, :], g_dram.rearrange("(k p) n -> p k n", p=P)).then_inc(g_in, 16)
                with nc.allow_non_contiguous_dma(reason="small parameters, channels to partitions"):
                    sp.dma_start(b[:, :], p["s5_b_glu"][0].rearrange("(k p) -> p k", p=P)).then_inc(b_in, 16)

            @block.tensor
            def _(pe):
                pe.wait_ge(w_in, 16)
                pe.wait_ge(g_in, 16)
                for m, (i, half) in enumerate(units):
                    if m >= 4:
                        pe.wait_ge(gate_done, m - 3)
                    for k in range(KG):
                        mm = pe.matmul(acc[m % 4][:, :], w[:, k, i * P:(i + 1) * P], g[:, k, half * 512:(half + 1) * 512],
                                       start=(k == 0), stop=(k == KG - 1))
                    mm.then_inc(ready, 1)

            @block.scalar
            def _(act):
                act.wait_ge(b_in, 16)
                for m, (i, half) in enumerate(units):
                    act.wait_ge(ready, m + 1)
                    if m >= 2:
                        act.wait_ge(out_done, m - 1)
                    nc.scalar.activation(gate[:, m % 2, :], acc[m % 4][:, :], ACT.Sigmoid, bias=b[:, i:i + 1]).then_inc(gate_done, 1)

            @block.vector
            def _(v):
                v.wait_ge(g_in, 16)
                for m, (i, half) in enumerate(units):
                    v.wait_ge(gate_done, m + 1)
                    t = slice(half * SUB // 2, (half + 1) * SUB // 2)
                    out = mix["qk"][:, i, CONV - 1:].rearrange("p (c t) -> p t c", t=SUB)[:, t, :]
                    v.tensor_tensor(out, g[:, i, half * 512:(half + 1) * 512].rearrange("p (t c) -> p t c", c=NCH),
                                    gate[:, m % 2, :].rearrange("p (t c) -> p t c", c=NCH), ALU.mult).then_inc(out_done, 1)


def project_out(nc, p, h2_dram, mix):
    with ExitStack() as ctx:
        sb, ps, sem = allocators(nc, ctx, "po_")
        HALF = 512
        RING = 3
        m_hi = sb("m_hi", [P, KD, T], F32R)
        m_lo = sb("m_lo", [P, KD, T], F32R)
        raw = sb("raw", [P, RING, HALF], F32)
        w_hi = sb("w_hi", [P, RING, HALF], F32R)
        w_lo = sb("w_lo", [P, RING, HALF], F32R)
        x = sb("x", [P, TT, HALF], F32)
        acc = [ps(f"acc{j}", [P, HALF], F32) for j in range(TT)]
        raw_full = [sem(f"raw_full{i}") for i in range(RING)]
        x_in = [sem(f"x_in{half}") for half in range(2)]
        m_hi_done, m_lo_done = sem("m_hi_done"), sem("m_lo_done")
        w_hi_done, w_lo_done = sem("w_hi_done"), sem("w_lo_done")
        used = sem("used")
        ready, added = sem("ready"), sem("added")
        h2_out = sem("h2_out")
        order = [4, 5, 6, 7, 0, 1, 2, 3]
        pieces = [(half, k) for half in range(2) for k in order]

        def source(k):
            return mix["sig_o"][:, k - 4, :] if k >= 4 else mix["qk"][:, k, CONV - 1:]

        w_out = p["w_out"][0].rearrange("(k p) n -> p k n", p=P)
        x_t = p["x"][0].rearrange("(j p) d -> p j d", p=P)
        h2_t = h2_dram.rearrange("(j p) d -> p j d", p=P)
        with nc.Block() as block:

            @block.sync
            def _(sp):
                for n, (half, k) in enumerate(pieces):
                    if n >= RING:
                        sp.wait_ge(w_lo_done, n - RING + 1)
                    sp.dma_start(raw[:, n % RING, :], w_out[:, k, half * HALF:(half + 1) * HALF]).then_inc(raw_full[n % RING], 16)
                    if n == 2:
                        sp.dma_start(x[:, :, :], x_t[:, :, 0:HALF]).then_inc(x_in[0], 16)
                for half in range(2):
                    for j in range(TT):
                        sp.wait_ge(added, half * TT + j + 1)
                        sp.dma_start(h2_t[:, j, half * HALF:(half + 1) * HALF], x[:, j, :]).then_inc(h2_out, 16)
                    if half == 0:
                        sp.wait_ge(h2_out, 16 * TT)
                        sp.dma_start(x[:, :, :], x_t[:, :, HALF:]).then_inc(x_in[1], 16)
                sp.wait_ge(h2_out, 16 * 2 * TT)

            @block.scalar
            def _(act):
                for n, (half, k) in enumerate(pieces):
                    if n < KD:
                        nc.scalar.copy(m_hi[:, k, :], source(k)).then_inc(m_hi_done, 1)
                    act.wait_ge(raw_full[n % RING], 16 * (n // RING + 1))
                    if n >= RING:
                        act.wait_ge(used, n - RING + 1)
                    nc.scalar.copy(w_hi[:, n % RING, :], raw[:, n % RING, :]).then_inc(w_hi_done, 1)

            @block.tensor
            def _(pe):
                for n, (half, k) in enumerate(pieces):
                    pe.wait_ge(w_lo_done, n + 1)
                    pe.wait_ge(m_lo_done, min(n + 1, KD))
                    first, last = n % KD == 0, n % KD == KD - 1
                    for j in range(TT):
                        toks = slice(j * P, (j + 1) * P)
                        if first and half:
                            pe.wait_ge(added, j + 1)
                        pe.matmul(acc[j][:, :], m_hi[:, k, toks], w_hi[:, n % RING, :], start=first, stop=False)
                        pe.matmul(acc[j][:, :], m_hi[:, k, toks], w_lo[:, n % RING, :], start=False, stop=False)
                        mm = pe.matmul(acc[j][:, :], m_lo[:, k, toks], w_hi[:, n % RING, :], start=False, stop=last)
                        if last and j < TT - 1:
                            mm.then_inc(ready, 1)
                    mm.then_inc(used, 1)

            @block.vector
            def _(v):
                def add(half):
                    v.wait_ge(x_in[half], 16)
                    for j in range(TT):
                        v.wait_ge(used, (half + 1) * KD) if j == TT - 1 else v.wait_ge(ready, half * (TT - 1) + j + 1)
                        v.tensor_tensor(x[:, j, :], x[:, j, :], acc[j][:, :], ALU.add).then_inc(added, 1)

                for n, (half, k) in enumerate(pieces):
                    if n < KD:
                        v.wait_ge(m_hi_done, n + 1)
                        v.tensor_tensor(m_lo[:, k, :], source(k), m_hi[:, k, :].bitcast(F32), ALU.subtract).then_inc(m_lo_done, 1)
                    v.wait_ge(w_hi_done, n + 1)
                    v.tensor_tensor(w_lo[:, n % RING, :], raw[:, n % RING, :], w_hi[:, n % RING, :].bitcast(F32),
                                    ALU.subtract).then_inc(w_lo_done, 1)
                    if n == KD:
                        add(0)
                add(1)
def route(nc, p, h2_dram, t_dram, keep):
    with ExitStack() as ctx:
        sb, ps, sem = allocators(nc, ctx, "rt_")
        h2 = sb("h2", [P, TT, D], F32)
        normed = sb("normed", [P, 2, D], F32)
        gain = sb("gain", [P, D], F32)
        tT = sb("tT", [P, 2, KD, P], F32)
        w_router = sb("w_router", [P, KD, E], F32)
        b_router = sb("b_router", [1, E], F32)
        b_down = sb("b_down", [E, D], F32)
        ident = sb("ident", [P, P], F32)
        ones_row = sb("ones_row", [1, P], F32)
        zero = sb("zero", [P, P], F32)
        square = sb("square", [P, D], F32)
        sumsq = sb("sumsq", [P, TT], F32)
        meansq = sb("meansq", [P, TT], F32)
        rstd = sb("rstd", [P, TT], F32)
        neg_half = sb("neg_half", [P, TT], F32)
        logits = sb("logits", [P, TT, E], F32)
        top_val = sb("top_val", [P, TT, 8], F32)
        top_idx = sb("top_idx", [P, TT, 8], U32)
        top_idxf = sb("top_idxf", [P, TT, K4], F32)
        shifted = sb("shifted", [P, TT, K4], F32)
        exps = sb("exps", [P, TT, K4], F32)
        exp_sum = sb("exp_sum", [P, TT], F32)
        inv_sum = sb("inv_sum", [P, TT], F32)
        iota_e = sb("iota_e", [P, E], F32)
        kplus1 = sb("kplus1", [P, K4], F32)
        onehot4 = sb("onehot4", [P, TT, K4, E], F32)
        weighted = sb("weighted", [P, TT, K4, E], F32)
        mask = sb("mask", [P, TT, E], F32)
        maskb = sb("maskb", [P, TT, E], BF16)
        kcol = sb("kcol", [P, TT, E], F32)
        dense_gate = sb("dense_gate", [P, TT, E], F32)
        gateT = sb("gateT", [E, TT, P], F32)
        part_id = sb("part_id", [P, 1], F32)
        before = sb("before", [P, P], BF16)
        onesb = sb("onesb", [P, P], BF16)
        h3 = sb("h3", [P, 2, D], F32)
        cnt_f = sb("cnt_f", [1, E], F32)
        waves = sb("waves", [1, WAVES - 1, E], F32)
        act_f = sb("act_f", [1, WAVES - 1, E], F32)
        ones_w = sb("ones_w", [1, (WAVES - 1) * E], F32)
        ord_f = sb("ord_f", [1, (WAVES - 1) * E], F32)
        ord_x = sb("ord_x", [1, (WAVES - 1) * E], F32)
        most = sb("most", [1, 1], F32)
        psT = [ps("psT0", [P, 512], F32), ps("psT1", [P, 512], F32)]
        psL = ps("psL", [P, 512], F32)
        psR = ps("psR", [P, 512], F32)
        psC = ps("psC", [P, 512], F32)
        psG = ps("psG", [P, 512], F32)
        psB = [ps("psB0", [P, 512], F32), ps("psB1", [P, 512], F32)]

        h2_in = sem("h2_in")
        consts_in = sem("consts_in")
        consts_set = sem("consts_set")
        squared = sem("squared")
        scaled = sem("scaled")
        normed_out = [sem("normed_out0"), sem("normed_out1")]
        turned = sem("turned")
        tT_set = sem("tT_set")
        logits_ready = sem("logits_ready")
        dve = sem("dve")
        rstd_set = sem("rstd_set")
        exp_ready = sem("exp_ready")
        mask_set = sem("mask_set")
        rank_ready = sem("rank_ready")
        gateT_ready = sem("gateT_ready")
        gateT_set = sem("gateT_set")
        bias_ready = sem("bias_ready")
        h3_out = [sem("h3_out0"), sem("h3_out1")]
        psB_read = sem("psB_read")

        h2_t = h2_dram.rearrange("(j p) d -> p j d", p=P)
        t_t = t_dram.rearrange("(j p) d -> p j d", p=P)
        CONSTS = 10 + WAVES - 1 + 4
        SHIFTED = 2 + 4 * TT
        with nc.Block() as block:

            @block.sync
            def _(sp):
                sp.dma_start(gain[:, :], p["norm_ffn_g"][0:1, :].to_broadcast([P, D])).then_inc(consts_in, 16)
                sp.dma_start(w_router[:, :, :], p["w_router"][0].rearrange("(k p) e -> p k e", p=P)).then_inc(consts_in, 16)
                sp.dma_start(b_router[:, :], p["b_router"][0:1, :]).then_inc(consts_in, 16)
                sp.dma_start(b_down[:, :], p["b_down"][0]).then_inc(consts_in, 16)
                for j in range(TT):
                    sp.dma_start(h2[:, j, :], h2_t[:, j, :]).then_inc(h2_in, 16)
                sp.wait_ge(h2_in, 16 * TT)
                for j in range(TT):
                    sp.wait_ge(scaled, j + 1)
                    sp.dma_start(t_t[:, j, :], normed[:, j % 2, :]).then_inc(normed_out[j % 2], 16)
                for j in range(TT):
                    sp.wait_ge(psB_read, 2 * j + 2)
                    sp.dma_start(h2_t[:, j, :], h3[:, j % 2, :]).then_inc(h3_out[j % 2], 16)
                for b in range(2):
                    sp.wait_ge(normed_out[b], 16 * TT // 2)
                    sp.wait_ge(h3_out[b], 16 * TT // 2)

            @block.gpsimd
            def _(pool):
                n = 0
                pool.memset(zero[:, :], 0.0).then_inc(consts_set, 1)
                pool.memset(ones_row[:, :], 1.0).then_inc(consts_set, 1)
                pool.memset(onesb[:, :], 1.0).then_inc(consts_set, 1)
                pool.memset(ones_w[:, :], 1.0).then_inc(consts_set, 1)
                pool.iota(iota_e[:, :], [[1, E]], base=0, channel_multiplier=0,
                          allow_small_or_imprecise_dtypes=True).then_inc(consts_set, 1)
                pool.iota(kplus1[:, :], [[1, K4]], base=1, channel_multiplier=0,
                          allow_small_or_imprecise_dtypes=True).then_inc(consts_set, 1)
                pool.iota(part_id[:, :], [[0, 1]], base=0, channel_multiplier=1,
                          allow_small_or_imprecise_dtypes=True).then_inc(consts_set, 1)
                pool.iota(keep["slot_no"][:, :], [[1, WAVES * SLOTS]], base=0, channel_multiplier=0,
                          allow_small_or_imprecise_dtypes=True).then_inc(consts_set, 1)
                pool.iota(keep["empty_at"][:, :], [[0, 1]], base=K4 * T + 1, channel_multiplier=1,
                          allow_small_or_imprecise_dtypes=True).then_inc(consts_set, 1)
                for w in range(WAVES - 1):
                    pool.memset(waves[:, w, :], float(SLOTS * (w + 1))).then_inc(consts_set, 1)
                pool.memset(neg_half[:, :], -0.5).then_inc(consts_set, 1)
                pool.wait_ge(consts_set, 10 + WAVES - 1)
                pool.affine_select(out=ident[:, :], in_=zero[:, :], compare_op=ALU.not_equal, fill=1.0, base=0,
                                   pattern=[[-1, P]], channel_multiplier=1).then_inc(consts_set, 1)
                pool.affine_select(out=before[:, :], in_=zero[:, :], compare_op=ALU.is_ge, fill=1.0, base=0,
                                   pattern=[[-1, P]], channel_multiplier=1).then_inc(consts_set, 1)
                pool.affine_select(out=keep["row_pick"][0:E, :], in_=zero[0:E, 0:E], compare_op=ALU.not_equal,
                                   fill=1.0, base=0, pattern=[[-1, E]], channel_multiplier=1).then_inc(consts_set, 1)
                pool.wait_ge(consts_set, CONSTS - 1)
                pool.affine_select(out=keep["row_pick"][E:2 * E, :], in_=zero[E:2 * E, 0:E], compare_op=ALU.not_equal,
                                   fill=1.0, base=0, pattern=[[-1, E]], channel_multiplier=1).then_inc(consts_set, 1)
                pool.wait_ge(consts_set, CONSTS)
                pool.wait_ge(dve, 1)
                pool.tensor_tensor(rstd[:, :], meansq[:, :], neg_half[:, :], ALU.pow).then_inc(rstd_set, 1)

            @block.scalar
            def _(act):
                for j in range(TT):
                    act.wait_ge(h2_in, 16 * TT)
                    if j:
                        act.wait_ge(squared, j)
                    nc.scalar.activation(square[:, :], h2[:, j, :], ACT.Square,
                                         accum_out=sumsq[:, j:j + 1]).then_inc(squared, 1)
                for n in range(2 * TT):
                    act.wait_ge(turned, n + 1)
                    if n >= 4:
                        act.wait_ge(logits_ready, n // 2 - 1)
                    nc.scalar.copy(tT[:, (n // 2) % 2, 4 * (n % 2):4 * (n % 2) + 4, :],
                                   psT[n % 2][:, :].rearrange("p (k t) -> p k t", k=4)).then_inc(tT_set, 1)
                act.wait_ge(dve, SHIFTED)
                nc.scalar.activation(exps[:, :, :], shifted[:, :, :], ACT.Exp).then_inc(exp_ready, 1)

            @block.tensor
            def _(pe):
                pe.wait_ge(consts_set, CONSTS)
                pe.wait_ge(consts_in, 64)
                for j in range(TT):
                    pe.wait_ge(scaled, j + 1)
                    for half in range(2):
                        n = 2 * j + half
                        if n >= 2:
                            pe.wait_ge(tT_set, n - 1)
                        for k in range(4):
                            mm = pe.transpose(psT[half][:, k * P:(k + 1) * P],
                                              normed[:, j % 2, (4 * half + k) * P:(4 * half + k + 1) * P], ident[:, :])
                        mm.then_inc(turned, 1)
                    pe.wait_ge(tT_set, 2 * j + 2)
                    for k in range(KD):
                        pe.matmul(psL[:, j * E:(j + 1) * E], tT[:, j % 2, k, :], w_router[:, k, :],
                                  start=(k == 0), stop=False)
                    pe.matmul(psL[:, j * E:(j + 1) * E], ones_row[:, :], b_router[:, :],
                              start=False, stop=True).then_inc(logits_ready, 1)
                pe.wait_ge(mask_set, 1)
                for j in range(TT):
                    for i in range(j + 1):
                        pe.matmul(psR[:, j * E:(j + 1) * E], before[:, :] if i == j else onesb[:, :], maskb[:, i, :],
                                  start=(i == 0), stop=(i == j))
                for i in range(TT):
                    mm = pe.matmul(psC[:, 0:E], onesb[:, :], maskb[:, i, :], start=(i == 0), stop=(i == TT - 1))
                mm.then_inc(rank_ready, 1)
                pe.wait_ge(mask_set, 2)
                for j in range(TT):
                    if j and j % 4 == 0:
                        pe.wait_ge(gateT_set, j // 4)
                    mm = pe.transpose(psG[0:E, (j % 4) * P:(j % 4 + 1) * P], dense_gate[:, j, :], ident[:, :])
                    if j % 4 == 3:
                        mm.then_inc(gateT_ready, 1)
                pe.wait_ge(gateT_set, 2)
                for j in range(TT):
                    for half in range(2):
                        n = 2 * j + half
                        if n >= 2:
                            pe.wait_ge(psB_read, n - 1)
                        pe.matmul(psB[half][:, :], gateT[:, j, :], b_down[:, half * 512:(half + 1) * 512],
                                  start=True, stop=True).then_inc(bias_ready, 1)

            @block.vector
            def _(v):
                count = [0]

                def link(ins):
                    count[0] += 1
                    ins.then_inc(dve, 1)
                    v.wait_ge(dve, count[0])

                v.wait_ge(squared, TT)
                link(v.tensor_scalar(meansq[:, :], sumsq[:, :], 1.0 / D, RMS_EPS, ALU.mult, ALU.add))
                v.wait_ge(rstd_set, 1)
                v.wait_ge(consts_in, 64)
                for j in range(TT):
                    if j >= 2:
                        v.wait_ge(normed_out[j % 2], 16 * (j // 2))
                        v.wait_ge(turned, 2 * (j - 1))
                    v.scalar_tensor_tensor(normed[:, j % 2, :], h2[:, j, :], rstd[:, j:j + 1], gain[:, :],
                                           ALU.mult, ALU.mult).then_inc(scaled, 1)
                v.wait_ge(logits_ready, TT)
                link(v.tensor_copy(logits[:, :, :], psL[:, 0:TT * E].rearrange("p (j e) -> p j e", j=TT)))
                for j in range(TT):
                    link(v.max(top_val[:, j, :], logits[:, j, :]))
                    link(v.max_index(top_idx[:, j, :], top_val[:, j, :], logits[:, j, :]))
                    link(v.tensor_copy(top_idxf[:, j, :], top_idx[:, j, 0:K4]))
                    link(v.tensor_scalar(shifted[:, j, :], top_val[:, j, 0:K4], top_val[:, j, 0:1], None,
                                         ALU.subtract))
                assert count[0] == SHIFTED
                v.wait_ge(consts_set, CONSTS)
                link(v.tensor_tensor(onehot4[:, :, :, :].rearrange("p j k e -> p (j k) e"),
                                     iota_e[:, :].unsqueeze(1).to_broadcast([P, TT * K4, E]),
                                     top_idxf[:, :, :].rearrange("p j k -> p (j k)").unsqueeze(2).to_broadcast([P, TT * K4, E]),
                                     ALU.is_equal))
                link(v.tensor_reduce(mask[:, :, :], onehot4[:, :, :, :].rearrange("p j k e -> p j e k"), AX.X, ALU.add))
                v.tensor_copy(maskb[:, :, :], mask[:, :, :]).then_inc(mask_set, 1)
                link(v.tensor_tensor(weighted[:, :, :, :], onehot4[:, :, :, :],
                                     kplus1[:, :].unsqueeze(1).unsqueeze(3).to_broadcast([P, TT, K4, E]), ALU.mult))
                link(v.tensor_reduce(kcol[:, :, :], weighted[:, :, :, :].rearrange("p j k e -> p j e k"), AX.X, ALU.add))
                v.wait_ge(exp_ready, 1)
                link(v.tensor_reduce(exp_sum[:, :], exps[:, :, :], AX.X, ALU.add))
                link(v.reciprocal(inv_sum[:, :], exp_sum[:, :]))
                link(v.tensor_tensor(keep["gates"][:, :, :], exps[:, :, :],
                                     inv_sum[:, :].unsqueeze(2).to_broadcast([P, TT, K4]), ALU.mult))
                link(v.tensor_tensor(weighted[:, :, :, :].rearrange("p j k e -> p (j k) e"),
                                     onehot4[:, :, :, :].rearrange("p j k e -> p (j k) e"),
                                     keep["gates"][:, :, :].rearrange("p j k -> p (j k)").unsqueeze(2).to_broadcast([P, TT * K4, E]),
                                     ALU.mult))
                v.tensor_reduce(dense_gate[:, :, :], weighted[:, :, :, :].rearrange("p j k e -> p j e k"), AX.X,
                                ALU.add).then_inc(mask_set, 1)
                picked = keep["picked"]
                v.tensor_scalar(picked[:, :, :, 0], mask[:, :, :], part_id[:, 0:1], None, ALU.mult)
                v.tensor_copy(picked[:, :, :, 1], kcol[:, :, :])
                for j in range(TT):
                    link(v.tensor_scalar(picked[:, j, :, 2], mask[:, j, :], float(j), None, ALU.mult))
                v.wait_ge(rank_ready, 1)
                link(v.tensor_copy(keep["rank"][:, :, :], psR[:, 0:TT * E].rearrange("p (j e) -> p j e", j=TT)))
                link(v.tensor_copy(cnt_f[:, :], psC[0:1, 0:E]))
                link(v.tensor_copy(keep["counts"][:, :], cnt_f[:, :]))
                link(v.tensor_reduce(most[:, :], cnt_f[:, :], AX.X, ALU.max))
                link(v.tensor_copy(keep["most"][:, :], most[:, :]))
                link(v.tensor_tensor(act_f[:, :, :], cnt_f[:, :].unsqueeze(1).to_broadcast([1, WAVES - 1, E]),
                                     waves[:, :, :], ALU.is_gt))
                acts = act_f[:, :, :].rearrange("p w e -> p (w e)")
                link(v.tensor_tensor_scan(ord_f[:, :], ones_w[:, :], acts, 0.0, ALU.mult, ALU.add))
                link(v.tensor_tensor(ord_x[:, :], ord_f[:, :], acts, ALU.subtract))
                link(v.tensor_copy(keep["more"][:, :], acts))
                link(v.tensor_copy(keep["order"][:, :], ord_x[:, :]))
                for q in range(2):
                    v.wait_ge(gateT_ready, q + 1)
                    v.tensor_copy(gateT[:, 4 * q:4 * q + 4, :],
                                  psG[0:E, :].rearrange("p (j t) -> p j t", j=4)).then_inc(gateT_set, 1)
                for j in range(TT):
                    if j >= 2:
                        v.wait_ge(h3_out[j % 2], 16 * (j // 2))
                    for half in range(2):
                        v.wait_ge(bias_ready, 2 * j + half + 1)
                        cols = slice(half * 512, (half + 1) * 512)
                        ins = v.tensor_tensor(h3[:, j % 2, cols], psB[half][:, :], h2[:, j, cols], ALU.add)
                        ins.then_inc(psB_read, 1)


def experts(nc, p, t_dram, y_dram, keep):
    with ExitStack() as ctx:
        sb, ps, sem = allocators(nc, ctx, "ex_")
        raw = sb("raw", [P, RAW, 4, 512], F32)
        w_hi = sb("w_hi", [P, SPLIT, 4, 512], F32R)
        w_lo = sb("w_lo", [P, SPLIT, 4, 512], F32R)
        x_rows = sb("x_rows", [P, BLOCKS, D], F32)
        x_hi = sb("x_hi", [P, BLOCKS, KD, P], F32R)
        x_lo = sb("x_lo", [P, BLOCKS, KD, P], F32R)
        gate = sb("gate", [P, BLOCKS, 512], F32)
        sig = sb("sig", [P, BLOCKS, 512], F32)
        swish = sb("swish", [P, BLOCKS, 512], F32)
        lin = sb("lin", [P, BLOCKS, 512], F32)
        hidden = sb("hidden", [P, BLOCKS, 512], F32)
        h_hi = sb("h_hi", [P, BLOCKS, 8, P], F32R)
        h_lo = sb("h_lo", [P, BLOCKS, 8, P], F32R)
        y = sb("y", [P, BLOCKS, D], F32)
        onehot = sb("onehot", [P, TT, SLOTS], BF16)
        bias_hl = sb("bias_hl", [2 * E, 2 * F], F32R)
        pick = sb("pick", [2 * E, P], F32R)
        ident = sb("ident", [P, P], F32)
        tok3 = sb("tok3", [P, BLOCKS, 3], F32)
        tokf = sb("tokf", [P, BLOCKS], F32)
        place = sb("place", [P, BLOCKS], F32)
        empty = sb("empty", [P, BLOCKS], F32)
        gather_at = sb("gather_at", [P, BLOCKS], U32)
        scatter_next = sb("scatter_next", [P, BLOCKS], U32)
        scatter_at = sb("scatter_at", [P, BLOCKS], U32)
        warm = sb("warm", [P, 1], F32)
        passed = sb("passed", [P, 1], F32)
        warm2 = sb("warm2", [P, 1], F32)
        ps_g = [ps(f"ps_g{b}", [P, 512], F32) for b in range(BLOCKS)]
        ps_l = [ps(f"ps_l{b}", [P, 512], F32) for b in range(BLOCKS)]
        ps_t = [ps(f"ps_t{b}", [P, 512], F32) for b in range(2)]

        raw_full = [sem(f"raw_full{s}") for s in range(RAW)]
        hi_done = sem("hi_done")
        lo_done = sem("lo_done")
        chunk_used = sem("chunk_used")
        t_full = sem("t_full")
        t_hi = sem("t_hi")
        t_free = sem("t_free")
        gate_done = sem("gate_done")
        sig_done = sem("sig_done")
        swish_done = sem("swish_done")
        lin_read = sem("lin_read")
        hidden_done = sem("hidden_done")
        pick_set = sem("pick_set")
        onehot_done = sem("onehot_done")
        places_set = sem("places_set")
        scatter_set = sem("scatter_set")
        y_a_read = sem("y_a_read")
        y_b_read = sem("y_b_read")
        x_full = [sem(f"x_full{b}") for b in range(BLOCKS)]
        x_init = sem("x_init")
        y_free = [sem(f"y_free{b}") for b in range(BLOCKS)]
        passed_done = sem("passed_done")
        placing = sem("placing")
        bias_in = sem("bias_in")
        bias_hi_set = sem("bias_hi_set")
        bias_set = sem("bias_set")
        ident_set = sem("ident_set")

        w_up, w_down = p["w_up"][0], p["w_down"][0]

        def piece(e, j):
            if j < 8:
                w, half, rows = w_up, (j // 2) % 2 * F + (j // 4) * 512, (j % 2) * 4
            else:
                w, half, rows = w_down, (j % 2) * 512, (j // 2 - 4) * 4
            src = w[bass.ds(e, 1), rows * P:(rows + 4) * P, half:half + 512]
            return src.rearrange("a (k p) n -> p (a k) n", p=P)

        MAIN = E

        FILLS, FIRST = 14, 8
        FIRST_STEPS = {"place": 0, "x0": 2, "x1": 4, "x2": 6}
        AHEAD = {"place": 0, "h0": 2, "x0": 5, "h1": 7, "x1": 10, "x2": 12}
        LAST = {"h0": 0, "h1": 3}
        ALONE = {"place": 0, "x0": 2, "x1": 4, "x2": 6, "h0": 8, "h1": 11}

        def first_fill(n, steps):
            return n * FILLS + (0 if steps is ALONE or steps is FIRST_STEPS else FIRST)

        def high_count(n, steps, step, k):
            before = steps[step] - (2 if "place" in steps else 0)
            return n * (FILLS - 2) + (before + (k + 1) + (0 if steps is ALONE or steps is FIRST_STEPS else FIRST - 2))

        def more_items(eng, body):
            most = eng.value_load(keep["most"][0:1, 0:1], min_val=0, max_val=T)
            with eng.If(most > SLOTS):
                for w in range(1, WAVES):
                    with eng.Fori(0, E) as e:
                        at = (w - 1) * E
                        more = eng.value_load(keep["more"][0:1, bass.ds(e + at, 1)], min_val=0, max_val=1)
                        with eng.If(more > 0):
                            order = eng.value_load(keep["order"][0:1, bass.ds(e + at, 1)], min_val=0,
                                                   max_val=(WAVES - 1) * E - 1)
                            body(order + MAIN, e, w)

        def by_blocks(eng, e, body):
            count = eng.value_load(keep["counts"][0:1, bass.ds(e, 1)], min_val=0, max_val=T)
            with eng.If(count > P):
                with eng.If(count > 2 * P):
                    body(3)
                with eng.Else():
                    body(2)
            with eng.Else():
                body(1)

        with nc.Block() as block:

            @block.sync
            def _(sp):
                for b in range(BLOCKS):
                    sp.dma_start(x_rows[:, b, :], t_dram[0:P, :]).then_inc(x_init, 16)
                sp.dma_start(raw[0:E, 3, :, :].rearrange("p k n -> p (k n)"), p["b_up"][0]).then_inc(bias_in, 16)
                sp.dma_start(raw[E:2 * E, 3, :, :].rearrange("p k n -> p (k n)"), p["b_up"][0]).then_inc(bias_in, 16)

                def load(n, e, j, wait):
                    if wait:
                        sp.wait_ge(lo_done, n * CHUNKS + (j - RAW + 1))
                    sp.dma_start(raw[:, j % RAW, :, :], piece(e, j)).then_inc(raw_full[j % RAW], 16)

                for j in range(RAW):
                    if j == 3:
                        sp.wait_ge(bias_set, 1)
                    load(0, 0, j, False)
                with sp.Fori(0, E - 1) as e:
                    for j in range(RAW, CHUNKS + RAW):
                        ahead = j // CHUNKS
                        load(e + ahead, e + ahead, j % CHUNKS, True)
                for j in range(RAW, CHUNKS):
                    load(E - 1, E - 1, j, True)

                def item(n, e, w):
                    for j in range(CHUNKS):
                        load(n, e, j, True)

                more_items(sp, item)

            @block.gpsimd
            def _(pool):
                pool.memset(ident[:, :], 0.0).then_inc(ident_set, 1)
                pool.wait_ge(ident_set, 1)
                pool.affine_select(out=ident[:, :], in_=ident[:, :], compare_op=ALU.not_equal, fill=1.0, base=0,
                                   pattern=[[-1, P]], channel_multiplier=1).then_inc(ident_set, 1)

                last_token = pool.to_reg(T - 1)
                last_output = pool.to_reg(K4 * T - 1)

                def pass_on(turn):
                    if turn is not None:
                        pool.wait_ge(passed_done, turn)
                    pool.tensor_tensor(passed[:, :], ident[:, 0:1], ident[:, 0:1], ALU.add).then_inc(passed_done, 1)

                def gather(n, fills, turn):
                    pool.wait_ge(places_set, n + 1)
                    if fills is not None:
                        pool.wait_ge(t_full, fills)
                    pass_on(turn)
                    for b in range(BLOCKS):
                        pool.indirect_dma_start(
                            out=x_rows[:, b, :], out_offset=None, in_=t_dram,
                            in_offset=bass.IndirectOffsetOnAxis(ap=gather_at[:, b:b + 1], axis=0),
                            bounds_check=last_token, oob_is_err=False).then_inc(x_full[b], 16)

                def scatter(n, turn):
                    pool.wait_ge(scatter_set, n + 1)
                    pool.wait_ge(y_a_read, n + 2)
                    pool.wait_ge(y_b_read, n + 2)
                    pass_on(turn)
                    for b in range(BLOCKS):
                        pool.indirect_dma_start(
                            out=y_dram, out_offset=bass.IndirectOffsetOnAxis(ap=scatter_at[:, b:b + 1], axis=0),
                            in_=y[:, b, :], in_offset=None,
                            bounds_check=last_output, oob_is_err=False).then_inc(y_free[b], 16)

                def swishes(n, half):
                    pool.wait_ge(sig_done, n * 2 + (half + 1))
                    pool.tensor_tensor(swish[:, :, :], gate[:, :, :], sig[:, :, :], ALU.mult).then_inc(swish_done, 1)

                def item(n, ahead):
                    swishes(n, 0)
                    if ahead:
                        gather(n + 1, n * FILLS + FIRST, n * 2 + 1)
                    swishes(n, 1)
                    scatter(n, n * 2 + (2 if ahead else 1))

                for b in range(BLOCKS):
                    pool.dma_start(y[:, b, :], t_dram[0:P, :]).then_inc(y_free[b], 16)
                pool.wait_ge(ident_set, 2)
                pool.wait_ge(x_init, 16 * BLOCKS)
                gather(0, None, None)
                with pool.Fori(0, E - 1) as n:
                    item(n, True)
                item(E - 1, False)

                def later(n, e, w):
                    gather(n, n * FILLS, n * 2)
                    item(n, False)
                    for b in range(BLOCKS):
                        pool.wait_ge(y_free[b], n * 16 + 32)

                more_items(pool, later)
                for b in range(BLOCKS):
                    pool.wait_ge(y_free[b], 16 * (E + 1))

            @block.scalar
            def _(act):
                def hi(n, j, wait):
                    act.wait_ge(raw_full[j % RAW], n * (16 * CHUNKS // RAW) + 16 * (j // RAW + 1))
                    if wait:
                        act.wait_ge(chunk_used, n * CHUNKS + (j - SPLIT + 1))
                    nc.scalar.copy(w_hi[:, j % SPLIT, :, :], raw[:, j % RAW, :, :]).then_inc(hi_done, 1)

                def x_high(n, steps, b):
                    for half in range(2):
                        fill = steps[f"x{b}"] + half
                        act.wait_ge(t_full, first_fill(n, steps) + (fill + 1))
                        nc.scalar.copy(x_hi[:, b, 4 * half:4 * half + 4, :],
                                       ps_t[fill % 2][:, :].rearrange("p (k t) -> p k t", k=4)).then_inc(t_hi, 1)

                def h_high(n, steps, half, blocks):
                    for b in range(blocks):
                        fill = steps[f"h{half}"] + b
                        act.wait_ge(t_full, first_fill(n, steps) + (fill + 1))
                        nc.scalar.copy(h_hi[:, b, 4 * half:4 * half + 4, :],
                                       ps_t[fill % 2][:, :].rearrange("p (k t) -> p k t", k=4)).then_inc(
                                           t_hi, 1 if b < blocks - 1 else 1 + BLOCKS - blocks)

                def sigmoid(n, half, blocks):
                    act.wait_ge(gate_done, n * 2 + (half + 1))
                    for b in range(blocks):
                        ins = nc.scalar.activation(sig[:, b, :], gate[:, b, :], ACT.Sigmoid, scale=ALPHA)
                    ins.then_inc(sig_done, 1)

                def y_out(n, j, banks, col, read, blocks):
                    act.wait_ge(chunk_used, n * CHUNKS + (j + 1))
                    for b in range(blocks):
                        act.wait_ge(y_free[b], n * 16 + 16)
                        ins = nc.scalar.copy(y[:, b, col:col + 512], banks[b][:, :])
                    ins.then_inc(read, 1)

                def item(n, steps, blocks):
                    for j in range(CHUNKS):
                        if j + SPLIT < CHUNKS:
                            hi(n, j + SPLIT, True)
                        elif steps is AHEAD:
                            hi(n + 1, j + SPLIT - CHUNKS, True)
                        if j == 5:
                            h_high(n, steps, 0, blocks)
                        if j in (1, 5):
                            sigmoid(n, j // 4, blocks)
                        if j == 8 and steps is AHEAD:
                            x_high(n, steps, 0)
                        if j == 9:
                            h_high(n, steps, 1, blocks)
                        if j == 10:
                            if steps is AHEAD:
                                x_high(n, steps, 1)
                            y_out(n, 10, ps_g, 0, y_a_read, blocks)
                        if j == 11:
                            if steps is AHEAD:
                                x_high(n, steps, 2)
                            y_out(n, 11, ps_l, 512, y_b_read, blocks)

                act.wait_ge(bias_in, 32)
                nc.scalar.activation(warm[0:2 * E, :], raw[0:2 * E, 3, 0, 0:1], ACT.Sigmoid).then_inc(y_a_read, 1)
                nc.scalar.copy(warm2[0:2 * E, :], raw[0:2 * E, 3, 0, 0:1]).then_inc(y_b_read, 1)
                nc.scalar.copy(bias_hl[:, :], raw[0:2 * E, 3, :, :].rearrange("p k n -> p (k n)")).then_inc(bias_hi_set, 1)
                for j in range(SPLIT):
                    hi(0, j, False)
                for b in range(BLOCKS):
                    x_high(0, FIRST_STEPS, b)
                with act.Fori(0, E - 1) as n:
                    by_blocks(act, n, lambda blocks: item(n, AHEAD, blocks))
                by_blocks(act, E - 1, lambda blocks: item(E - 1, LAST, blocks))

                def later(n, e, w):
                    for j in range(SPLIT):
                        hi(n, j, True)
                    for b in range(BLOCKS):
                        x_high(n, ALONE, b)
                    item(n, ALONE, BLOCKS)

                more_items(act, later)

            @block.vector
            def _(v):
                def lo(n, j):
                    v.wait_ge(hi_done, n * CHUNKS + (j + 1))
                    v.tensor_tensor(w_lo[:, j % SPLIT, :, :], raw[:, j % RAW, :, :],
                                    w_hi[:, j % SPLIT, :, :].bitcast(F32), ALU.subtract).then_inc(lo_done, 1)

                def x_low(n, steps, b):
                    for half in range(2):
                        fill = steps[f"x{b}"] + half
                        v.wait_ge(t_hi, high_count(n, steps, f"x{b}", half))
                        rows = slice(4 * half, 4 * half + 4)
                        v.tensor_tensor(x_lo[:, b, rows, :], ps_t[fill % 2][:, :].rearrange("p (k t) -> p k t", k=4),
                                        x_hi[:, b, rows, :].bitcast(F32), ALU.subtract).then_inc(t_free, 1)

                def h_low(n, steps, half, blocks):
                    for b in range(blocks):
                        fill = steps[f"h{half}"] + b
                        last = b == blocks - 1
                        v.wait_ge(t_hi, high_count(n, steps, f"h{half}", b))
                        rows = slice(4 * half, 4 * half + 4)
                        v.tensor_tensor(h_lo[:, b, rows, :], ps_t[fill % 2][:, :].rearrange("p (k t) -> p k t", k=4),
                                        h_hi[:, b, rows, :].bitcast(F32), ALU.subtract).then_inc(
                                            t_free, 1 + BLOCKS - blocks if last else 1)

                def find(e, w):
                    for j in range(TT):
                        ins = v.tensor_scalar(onehot[:, j, :], keep["slot_no"][:, w * SLOTS:(w + 1) * SLOTS],
                                              keep["rank"][:, j, bass.ds(e, 1)], None, ALU.is_equal)
                    ins.then_inc(onehot_done, 1)

                def choose(n, e):
                    v.tensor_copy(pick[:, :], keep["row_pick"][:, bass.ds(e, 1)].to_broadcast([2 * E, P])).then_inc(pick_set, 1)

                def places(n, steps):
                    v.wait_ge(t_full, first_fill(n, steps) + (steps["place"] + 2))
                    v.tensor_copy(tok3[:, :, :], ps_t[0][:, 0:3 * BLOCKS].rearrange("p (b c) -> p b c", b=BLOCKS)).then_inc(t_free, 2)
                    v.wait_ge(t_free, first_fill(n, steps) + (steps["place"] + 2))
                    v.scalar_tensor_tensor(tokf[:, :], tok3[:, :, 2], float(P), tok3[:, :, 0], ALU.mult, ALU.add)
                    v.scalar_tensor_tensor(empty[:, :], tok3[:, :, 1], 0.0,
                                           keep["empty_at"][:, 0:1].to_broadcast([P, BLOCKS]),
                                           ALU.is_equal, ALU.mult).then_inc(placing, 1)

                def store_places(n, m):
                    v.wait_ge(placing, 3 * m + 1)
                    v.scalar_tensor_tensor(place[:, :], tokf[:, :], float(K4), tok3[:, :, 1], ALU.mult, ALU.add).then_inc(placing, 1)
                    v.tensor_copy(gather_at[:, :], tokf[:, :])
                    v.wait_ge(placing, 3 * m + 2)
                    v.scalar_tensor_tensor(place[:, :], place[:, :], -1.0, empty[:, :], ALU.add, ALU.add).then_inc(placing, 1)
                    v.wait_ge(placing, 3 * m + 3)
                    v.tensor_copy(scatter_next[:, :], place[:, :]).then_inc(places_set, 1)

                def keep_places(n):
                    for b in range(BLOCKS):
                        v.wait_ge(y_free[b], n * 16 + 16)
                    v.wait_ge(places_set, n + 1)
                    v.tensor_copy(scatter_at[:, :], scatter_next[:, :]).then_inc(scatter_set, 1)

                def clamp_gate(n, half, j, blocks):
                    v.wait_ge(chunk_used, n * CHUNKS + (j + 1))
                    for b in range(blocks):
                        ins = v.tensor_scalar(gate[:, b, :], ps_g[b][:, :], LIMIT, None, ALU.min)
                    ins.then_inc(gate_done, 1)

                def hide(n, half, j, blocks):
                    v.wait_ge(chunk_used, n * CHUNKS + (j + 1))
                    for b in range(blocks):
                        ins = v.tensor_scalar(lin[:, b, :], ps_l[b][:, :], LIMIT, -LIMIT, ALU.min, ALU.max)
                    ins.then_inc(lin_read, 1)
                    v.wait_ge(swish_done, n * 2 + (half + 1))
                    v.wait_ge(lin_read, n * 2 + (half + 1))
                    for b in range(blocks):
                        ins = v.scalar_tensor_tensor(hidden[:, b, :], lin[:, b, :], 1.0, swish[:, b, :], ALU.add, ALU.mult)
                    ins.then_inc(hidden_done, 1)

                def item(n, steps, blocks, e=None, w=0):
                    for j in range(CHUNKS):
                        if j + SPLIT < CHUNKS:
                            lo(n, j + SPLIT)
                        elif steps is AHEAD:
                            lo(n + 1, j + SPLIT - CHUNKS)
                        if j == 0 and steps is AHEAD:
                            find(n + 1, 0)
                        if j == 1:
                            clamp_gate(n, 0, 1, blocks)
                        if j == 2:
                            keep_places(n)
                            if steps is AHEAD:
                                places(n, steps)
                                store_places(n + 1, n + 1)
                        if j == 3:
                            hide(n, 0, 3, blocks)
                        if j == 5:
                            h_low(n, steps, 0, blocks)
                            clamp_gate(n, 1, 5, blocks)
                        if j == 7:
                            hide(n, 1, 7, blocks)
                            if steps is AHEAD:
                                choose(n + 1, n + 1)
                        if j == 8 and steps is AHEAD:
                            x_low(n, steps, 0)
                        if j == 9:
                            h_low(n, steps, 1, blocks)
                        if j == 10 and steps is AHEAD:
                            x_low(n, steps, 1)
                        if j == 11 and steps is AHEAD:
                            x_low(n, steps, 2)

                v.memset(gate[:, :, :], 0.0)
                v.memset(sig[:, :, :], 0.0)
                v.wait_ge(bias_hi_set, 1)
                v.tensor_tensor(bias_hl[E:2 * E, :], raw[E:2 * E, 3, :, :].rearrange("p k n -> p (k n)"),
                                bias_hl[E:2 * E, :].bitcast(F32), ALU.subtract).then_inc(bias_set, 1)
                find(0, 0)
                choose(0, 0)
                for j in range(SPLIT):
                    lo(0, j)
                places(0, FIRST_STEPS)
                store_places(0, 0)
                for b in range(BLOCKS):
                    x_low(0, FIRST_STEPS, b)
                with v.Fori(0, E - 1) as n:
                    by_blocks(v, n, lambda blocks: item(n, AHEAD, blocks))
                by_blocks(v, E - 1, lambda blocks: item(E - 1, LAST, blocks))

                def later(n, e, w):
                    find(e, w)
                    choose(n, e)
                    for j in range(SPLIT):
                        lo(n, j)
                    places(n, ALONE)
                    store_places(n, n)
                    for b in range(BLOCKS):
                        x_low(n, ALONE, b)
                    item(n, ALONE, BLOCKS)

                more_items(v, later)

            @block.tensor
            def _(pe):
                def place_matmuls(n, steps, e):
                    pe.wait_ge(onehot_done, n + (1 if steps is not AHEAD else 2))
                    fill = steps["place"]
                    first = first_fill(n, steps)
                    if steps is not FIRST_STEPS:
                        pe.wait_ge(t_free, first + (fill - 1))
                    for b in range(BLOCKS):
                        for j in range(TT):
                            mm = pe.matmul(ps_t[0][:, 3 * b:3 * b + 3], onehot[:, j, b * P:(b + 1) * P],
                                           keep["picked"][:, j, bass.ds(e, 1), :].rearrange("p a c -> p (a c)"),
                                           start=(j == 0), stop=(j == TT - 1))
                    mm.then_inc(t_full, 2)

                def bank(n, steps, fill):
                    if steps is not FIRST_STEPS or fill > 1:
                        pe.wait_ge(t_free, first_fill(n, steps) + (fill - 1))
                    return ps_t[fill % 2]

                def x_turn(n, steps, b):
                    pe.wait_ge(x_full[b], n * 16 + (16 if steps is not AHEAD else 32))
                    for half in range(2):
                        to = bank(n, steps, steps[f"x{b}"] + half)
                        for k in range(4):
                            mm = pe.transpose(to[:, k * P:(k + 1) * P],
                                              x_rows[:, b, (4 * half + k) * P:(4 * half + k + 1) * P], ident[:, :])
                        mm.then_inc(t_full, 1)

                def h_turn(n, steps, half, blocks):
                    pe.wait_ge(hidden_done, n * 2 + (half + 1))
                    for b in range(blocks):
                        to = bank(n, steps, steps[f"h{half}"] + b)
                        for k in range(4):
                            mm = pe.transpose(to[:, k * P:(k + 1) * P], hidden[:, b, k * P:(k + 1) * P], ident[:, :])
                        mm.then_inc(t_full, 1 if b < blocks - 1 else 1 + BLOCKS - blocks)

                def multiply(n, j, blocks):
                    pe.wait_ge(lo_done, n * CHUNKS + (j + 1))
                    s = j % SPLIT
                    up = j < 8
                    part = j % 2 if up else j // 2 - 4
                    if up:
                        banks = (ps_g, ps_l)[(j // 2) % 2]
                        hi_in, lo_in = x_hi, x_lo
                    else:
                        banks = (ps_g, ps_l)[j % 2]
                        hi_in, lo_in = h_hi, h_lo
                    if j in (0, 2):
                        pe.wait_ge((y_a_read, y_b_read)[j // 2], n + 1)
                    elif j in (4, 8):
                        pe.wait_ge(gate_done, n * 2 + j // 4)
                    elif j in (6, 9):
                        pe.wait_ge(lin_read, n * 2 + (j // 3 - 1))
                    if j == 0:
                        pe.wait_ge(pick_set, n + 1)
                    for b in range(blocks):
                        if up and part == 0:
                            col = (j // 2) % 2 * F + (j // 4) * 512
                            pe.matmul(banks[b][:, :], pick[:, :], bias_hl[:, col:col + 512], start=True, stop=False)
                        for k in range(4):
                            kk = 4 * part + k
                            first = (not up) and kk == 0
                            last = part == 1 and k == 3
                            pe.matmul(banks[b][:, :], hi_in[:, b, kk, :], w_hi[:, s, k, :], start=first, stop=False)
                            pe.matmul(banks[b][:, :], hi_in[:, b, kk, :], w_lo[:, s, k, :], start=False, stop=False)
                            mm = pe.matmul(banks[b][:, :], lo_in[:, b, kk, :], w_hi[:, s, k, :], start=False, stop=last)
                    mm.then_inc(chunk_used, 1)

                def item(n, steps, blocks):
                    for j in range(CHUNKS):
                        if j == 0:
                            pe.wait_ge(t_free, n * FILLS + FIRST_STEPS[f"x{blocks - 1}"] + 2)
                        if j in (8, 10):
                            pe.wait_ge(t_free, first_fill(n, steps) + (steps[f"h{j // 2 - 4}"] + BLOCKS))
                        multiply(n, j, blocks)
                        if j == 2 and steps is AHEAD:
                            place_matmuls(n, steps, n + 1)
                        if j == 5:
                            h_turn(n, steps, 0, blocks)
                        if j == 8 and steps is AHEAD:
                            x_turn(n, steps, 0)
                        if j == 9:
                            h_turn(n, steps, 1, blocks)
                        if j == 10 and steps is AHEAD:
                            x_turn(n, steps, 1)
                        if j == 11 and steps is AHEAD:
                            x_turn(n, steps, 2)

                pe.wait_ge(ident_set, 2)
                pe.wait_ge(bias_set, 1)
                place_matmuls(0, FIRST_STEPS, 0)
                for b in range(BLOCKS):
                    x_turn(0, FIRST_STEPS, b)
                with pe.Fori(0, E - 1) as n:
                    by_blocks(pe, n, lambda blocks: item(n, AHEAD, blocks))
                by_blocks(pe, E - 1, lambda blocks: item(E - 1, LAST, blocks))

                def later(n, e, w):
                    place_matmuls(n, ALONE, e)
                    for b in range(BLOCKS):
                        x_turn(n, ALONE, b)
                    item(n, ALONE, BLOCKS)

                more_items(pe, later)


def finish(nc, p, h3_dram, y_dram, out, keep):
    with ExitStack() as ctx:
        sb, ps, sem = allocators(nc, ctx, "fi_")
        gain = sb("gain", [P, D], F32)
        h3 = sb("h3", [P, TT, D], F32)
        ys = sb("ys", [P, 4, K4, D], F32)
        square = sb("square", [P, D], F32)
        sumsq = sb("sumsq", [P, TT], F32)
        meansq = sb("meansq", [P, TT], F32)
        rstd = sb("rstd", [P, TT], F32)
        neg_half = sb("neg_half", [P, 1], F32)
        result = sb("result", [P, TT, D], F32)
        gain_in = sem("gain_in")
        h3_in = [sem(f"h3_in{j}") for j in range(TT)]
        ys_in = [sem(f"ys_in{b}") for b in range(4)]
        summed = sem("summed")
        squared = sem("squared")
        dve = sem("dve")
        exponent_set = sem("exponent_set")
        mean_set = sem("mean_set")
        rstd_set = sem("rstd_set")
        result_set = sem("result_set")
        stored = sem("stored")
        h3_t = h3_dram.rearrange("(j p) d -> p j d", p=P)
        y_t = y_dram.rearrange("(j p k) d -> p j k d", p=P, k=K4)
        out_t = out[0].rearrange("(j p) d -> p j d", p=P)
        with nc.Block() as block:

            @block.sync
            def _(sp):
                for j in range(TT):
                    sp.dma_start(h3[:, j, :], h3_t[:, j, :]).then_inc(h3_in[j], 16)
                    if j >= 4:
                        sp.wait_ge(summed, j - 3)
                    sp.dma_start(ys[:, j % 4, :, :], y_t[:, j, :, :]).then_inc(ys_in[j % 4], 16)
                    if j == 0:
                        sp.dma_start(gain[:, :], p["norm_final_g"].rearrange("(a d) -> a d", a=1).to_broadcast([P, D])).then_inc(gain_in, 16)
                for j in range(TT):
                    sp.wait_ge(result_set, j + 1)
                    sp.dma_start(out_t[:, j, :], result[:, j, :]).then_inc(stored, 16)
                sp.wait_ge(stored, 16 * TT)

            @block.gpsimd
            def _(pool):
                pool.memset(neg_half[:, :], -0.5).then_inc(exponent_set, 1)
                pool.wait_ge(exponent_set, 1)
                for j in range(TT):
                    pool.wait_ge(mean_set, j + 1)
                    pool.tensor_tensor(rstd[:, j:j + 1], meansq[:, j:j + 1], neg_half[:, :], ALU.pow).then_inc(rstd_set, 1)

            @block.scalar
            def _(act):
                for j in range(TT):
                    act.wait_ge(summed, j + 1)
                    if j:
                        act.wait_ge(squared, j)
                    nc.scalar.activation(square[:, :], h3[:, j, :], ACT.Square, accum_out=sumsq[:, j:j + 1]).then_inc(squared, 1)

            @block.vector
            def _(v):
                count = [0]

                def link(ins):
                    count[0] += 1
                    ins.then_inc(dve, 1)
                    v.wait_ge(dve, count[0])

                def normalise(j):
                    v.wait_ge(squared, j + 1)
                    v.tensor_scalar(meansq[:, j:j + 1], sumsq[:, j:j + 1], 1.0 / D, RMS_EPS, ALU.mult, ALU.add).then_inc(mean_set, 1)

                def scale(j):
                    v.wait_ge(rstd_set, j + 1)
                    v.scalar_tensor_tensor(result[:, j, :], h3[:, j, :], rstd[:, j:j + 1], gain[:, :],
                                           ALU.mult, ALU.mult).then_inc(result_set, 1)

                v.wait_ge(gain_in, 16)
                for j in range(TT):
                    v.wait_ge(h3_in[j], 16)
                    v.wait_ge(ys_in[j % 4], 16 * (j // 4 + 1))
                    for k in range(K4):
                        ins = v.scalar_tensor_tensor(h3[:, j, :], ys[:, j % 4, k, :], keep["gates"][:, j, k:k + 1],
                                                     h3[:, j, :], ALU.mult, ALU.add)
                        if k < K4 - 1:
                            link(ins)
                    ins.then_inc(summed, 1)
                    if j:
                        normalise(j - 1)
                    if j > 1:
                        scale(j - 2)
                scale(TT - 2)
                normalise(TT - 1)
                scale(TT - 1)


def hybrid_block(nc, p, out):
    def dram(name, shape):
        return nc.dram_tensor(name, shape, F32, kind="Internal").ap()

    u = dram("u", [S5W, T])
    g = dram("g", [S5W, T])
    h2 = dram("h2", [T, D])
    t = dram("t", [T, D])
    y = dram("y", [K4 * T, D])
    with ExitStack() as ctx:
        mix = mixer_tiles(nc, ctx)
        project(nc, p, u, mix)
        mlstm(nc, p, mix)
        s5(nc, p, u, g, mix)
        project_out(nc, p, h2, mix)
    with ExitStack() as ctx:
        keep = keep_tiles(nc, ctx)
        route(nc, p, h2, t, keep)
        experts(nc, p, t, y, keep)
        finish(nc, p, h2, y, out, keep)


_INS = ["x", "norm_mix_g", "w_in", "s5_log_dt", "s5_a_re", "s5_a_im", "s5_b_re", "s5_b_im", "s5_c_re", "s5_c_im",
        "s5_d", "s5_w_glu", "s5_b_glu", "ml_conv_w", "ml_conv_b", "ml_b_gates", "ml_norm_g", "w_out", "norm_ffn_g",
        "w_router", "b_router", "w_up", "b_up", "w_down", "b_down", "norm_final_g"]


def kernel(**inputs):
    import numpy as _np
    import concourse.bacc as _bacc
    from concourse import mybir as _mybir
    from concourse.bass_utils import run_bass_kernel_spmd as _run

    nc = _bacc.Bacc("TRN2", target_bir_lowering=False, num_devices=1)
    arrays, params = {}, {}
    for name in _INS:
        a = _np.ascontiguousarray(inputs[name])
        arrays[f"in_{name}_dram"] = a
        params[name] = nc.dram_tensor(f"in_{name}_dram", a.shape, _mybir.dt.from_np(a.dtype), kind="ExternalInput").ap()
    out = nc.dram_tensor("out_0_dram", (1, T, D), _mybir.dt.from_np(_np.dtype("float32")), kind="ExternalOutput").ap()
    hybrid_block(nc, params, out)
    r = _run(nc, [arrays], core_ids=[0])
    return r.results[0]["out_0_dram"]
```
